# Optimizing a Trainium2 kernel written in Bass

```python
import functools
import jax, jax.numpy as jnp
from jax import lax
import numpy as np

D_MODEL = 2048
BATCH = 1
SEQ = 256
DEPTH = 1
DEC_BATCH = 8
DEC_SEQ = 4
PAST_LEN = 1024
PAGE_SIZE = 128

HEAD_DIM_A = 128
N_HEADS_A = D_MODEL // 256
C_A = N_HEADS_A * HEAD_DIM_A
IDX_HEADS = 8
IDX_DIM = 64
TOPK_MAX = 256
Q_BLOCK = 32
HEAD_B = 64
N_HEADS_B = D_MODEL // 128
C_B = N_HEADS_B * HEAD_B
D_DECAY = 64
D_AAA = 64
D_GATE = 160
LNX_EPS = 64e-5
D_FF = -(-8 * D_MODEL // (3 * 256)) * 256
ROPE_THETA = 500000.0
ROPE_FRACTION = 4
NORM_EPS = 1e-6
COLS_A = [C_A, C_A, C_A, IDX_HEADS * IDX_DIM, IDX_DIM, IDX_HEADS, D_MODEL, D_MODEL]
COLS_B = [C_B, C_B, C_B, D_DECAY, D_AAA, D_GATE]
N_IN_A = 3 * C_A + IDX_HEADS * IDX_DIM + IDX_DIM + IDX_HEADS + 2 * D_MODEL
N_IN_B = 3 * C_B + D_DECAY + D_AAA + D_GATE

kernel_name = 'hybrid_dsa_rwkv7_decoder_step'

def _rmsnorm(x, g):
    xf = x.astype(jnp.float32)
    y = xf * lax.rsqrt(jnp.mean(xf * xf, axis=-1, keepdims=True) + NORM_EPS)
    return (y * g.astype(jnp.float32)).astype(x.dtype)

def _split_last(t, sizes):
    out, o = [], 0
    for s in sizes:
        out.append(t[..., o:o + s])
        o += s
    return out

def _rope(x, pos):
    d = x.shape[-1]
    rot = d // ROPE_FRACTION
    half = rot // 2
    inv = ROPE_THETA ** (-jnp.arange(half, dtype=jnp.float32) * 2.0 / rot)
    ang = pos.astype(jnp.float32)[:, None] * inv[None, :]
    cos = jnp.cos(ang)[:, None, :].astype(x.dtype)
    sin = jnp.sin(ang)[:, None, :].astype(x.dtype)
    x1, x2 = x[..., :half], x[..., half:rot]
    return jnp.concatenate([x1 * cos - x2 * sin, x2 * cos + x1 * sin, x[..., rot:]], axis=-1)

def _gather_rows(src, idx):
    return jax.vmap(lambda s, i: s[i])(src, idx)

def _indexer_scores(qi, wi, ki):
    logits = jnp.einsum('bthd,bsd->bths', qi, ki).astype(jnp.float32)
    return jnp.einsum('bths,bth->bts', jax.nn.relu(logits), wi.astype(jnp.float32))

def _select(scores, q_pos, n_sel):
    L = scores.shape[-1]
    future = jnp.arange(L)[None, None, :] > q_pos[None, :, None]
    s = jnp.where(future, -1e30, scores)
    _, idx = lax.top_k(s, n_sel)
    return idx, idx <= q_pos[None, :, None]

def _attend(q, k_sel, v_sel, valid):
    s = jnp.einsum('bthd,btkhd->bthk', q, k_sel).astype(jnp.float32) * (HEAD_DIM_A ** -0.5)
    s = jnp.where(valid[:, :, None, :], s, -1e30)
    p = jax.nn.softmax(s, axis=-1).astype(v_sel.dtype)
    return jnp.einsum('bthk,btkhd->bthd', p, v_sel)

def _attn_prompt(q, k, v, qi, ki, wi):
    B, S = q.shape[:2]
    n_sel = min(TOPK_MAX, S // 4)
    qb = min(Q_BLOCK, S)
    nb = S // qb

    def to_blocks(t):
        return jnp.moveaxis(t.reshape((B, nb, qb) + t.shape[2:]), 1, 0)

    def block(args):
        q_b, qi_b, wi_b, start = args
        q_pos = start + jnp.arange(qb)
        idx, valid = _select(_indexer_scores(qi_b, wi_b, ki), q_pos, n_sel)
        return _attend(q_b, _gather_rows(k, idx), _gather_rows(v, idx), valid)

    out = lax.map(block, (to_blocks(q), to_blocks(qi), to_blocks(wi), jnp.arange(nb) * qb))
    return jnp.moveaxis(out, 0, 1).reshape(q.shape)

def _attn_sample(q, k, v, qi, ki, wi, cache_k, cache_v, cache_ki, page_table, layer):
    B, T = q.shape[:2]
    past = page_table.shape[1] * PAGE_SIZE
    n_sel = min(TOPK_MAX, (past + T) // 4)
    ki_past = cache_ki[layer, page_table].reshape(B, past, IDX_DIM).astype(ki.dtype)
    ki_all = jnp.concatenate([ki_past, ki], axis=1)
    q_pos = past + jnp.arange(T)
    idx, valid = _select(_indexer_scores(qi, wi, ki_all), q_pos, n_sel)
    in_past = (idx < past)[..., None, None]
    pidx = jnp.minimum(idx, past - 1)
    phys_page = jax.vmap(lambda pt, pg: pt[pg])(page_table, pidx // PAGE_SIZE)
    slot = pidx % PAGE_SIZE
    nidx = jnp.clip(idx - past, 0, T - 1)
    k_sel = jnp.where(in_past, cache_k[layer, phys_page, slot].astype(k.dtype), _gather_rows(k, nidx))
    v_sel = jnp.where(in_past, cache_v[layer, phys_page, slot].astype(v.dtype), _gather_rows(v, nidx))
    return _attend(q, k_sel, v_sel, valid)

def _rwkv7(pb, pb_prev, wkv0, p):
    B, T, _ = pb.shape
    f32 = jnp.float32
    xm = pb + (pb_prev - pb) * p['mu_b']
    r, k, v, xw, xa, xg = _split_last(xm, COLS_B)
    w = -jax.nn.softplus(-(p['w0'] + jnp.tanh(xw) @ p['w2'])) - 0.5
    decay = jnp.exp(-jnp.exp(w.astype(f32)))
    a = jax.nn.sigmoid(p['a0'] + xa @ p['a2'])
    g = jax.nn.sigmoid(xg) @ p['g2']
    heads = lambda t: t.reshape(B, T, N_HEADS_B, HEAD_B).astype(f32)
    kk = heads(k * p['k_k'])
    kk = kk / jnp.maximum(jnp.linalg.norm(kk, axis=-1, keepdims=True), 1e-12)
    k = k * (1 + (a - 1) * p['k_a'])
    r_h, k_h, v_h, a_h, dec_h = heads(r), heads(k), heads(v), heads(a), heads(decay)

    def step(S, inp):
        r_t, dec_t, k_t, v_t, a_t, b_t = inp
        sa = jnp.einsum('bhij,bhj->bhi', S, a_t)
        S = S * dec_t[:, :, None, :] + sa[..., None] * b_t[:, :, None, :] + v_t[..., None] * k_t[:, :, None, :]
        return S, jnp.einsum('bhij,bhj->bhi', S, r_t)

    tm = lambda t: jnp.moveaxis(t, 1, 0)
    S_T, y = lax.scan(step, wkv0.astype(f32),
                      (tm(r_h), tm(dec_h), tm(k_h), tm(v_h), tm(-kk), tm(kk * a_h)))
    y = jnp.moveaxis(y, 0, 1)
    mean = jnp.mean(y, axis=-1, keepdims=True)
    var = jnp.mean(jnp.square(y - mean), axis=-1, keepdims=True)
    yn = ((y - mean) * lax.rsqrt(var + LNX_EPS)).reshape(B, T, C_B) * p['lnx_w'] + p['lnx_b']
    bonus = (jnp.sum(r_h * k_h * p['r_k'], axis=-1, keepdims=True) * v_h).reshape(B, T, C_B)
    out = ((yn + bonus) * g).astype(pb.dtype)
    return out, S_T.astype(wkv0.dtype)

def _layer(x, h_prev, wkv0, pos0, attn_fn, p):
    B, T, _ = x.shape
    h = _rmsnorm(x, p['g_mix'])
    proj = h @ p['w_in']
    qa, ka, va, qi, ki, wi, ga, gb = _split_last(proj[..., :N_IN_A], COLS_A)
    pos = pos0 + jnp.arange(T)
    qa = _rope(qa.reshape(B, T, N_HEADS_A, HEAD_DIM_A), pos)
    ka = _rope(ka.reshape(B, T, N_HEADS_A, HEAD_DIM_A), pos)
    va = va.reshape(B, T, N_HEADS_A, HEAD_DIM_A)
    qi = _rope(qi.reshape(B, T, IDX_HEADS, IDX_DIM), pos)
    ki = _rope(ki.reshape(B, T, 1, IDX_DIM), pos)[:, :, 0]
    wi = wi * (IDX_HEADS ** -0.5 * IDX_DIM ** -0.5)
    o_a = attn_fn(qa, ka, va, qi, ki, wi).reshape(B, T, C_A)
    pb = proj[..., N_IN_A:]
    pb_first = h_prev @ p['w_in'][:, N_IN_A:]
    pb_prev = jnp.concatenate([pb_first[:, None, :], pb[:, :-1]], axis=1)
    o_b, wkv = _rwkv7(pb, pb_prev, wkv0, p)
    mixed = jax.nn.sigmoid(ga) * (o_a @ p['w_pa']) + jax.nn.sigmoid(gb) * (o_b @ p['w_pb'])
    x = x + mixed @ p['w_o']
    h2 = _rmsnorm(x, p['g_ffn'])
    x = x + (jax.nn.silu(h2 @ p['w_gate']) * (h2 @ p['w_up'])) @ p['w_down']
    return x, ka, va, ki, wkv, h[:, -1]

def setup_inputs(seed: int = 0) -> dict:
    key = jax.random.key(seed)
    ks = jax.random.split(key, 32)
    f32 = jnp.float32
    nrm = lambda k, shape, scale: scale * jax.random.normal(k, shape, f32)
    n_pages = PAST_LEN // PAGE_SIZE
    n_used = DEC_BATCH * n_pages
    n_pool = n_used + max(1, n_used // 4)
    page_table = jax.random.permutation(ks[7], n_pool)[:n_used].reshape(DEC_BATCH, n_pages).astype(jnp.int32)
    return {
        'x_prompt': nrm(ks[0], (BATCH, SEQ, D_MODEL), 1.0),
        'x_sample': nrm(ks[1], (DEC_BATCH, DEC_SEQ, D_MODEL), 1.0),
        'cache_k': nrm(ks[2], (DEPTH, n_pool, PAGE_SIZE, N_HEADS_A, HEAD_DIM_A), 1.0),
        'cache_v': nrm(ks[3], (DEPTH, n_pool, PAGE_SIZE, N_HEADS_A, HEAD_DIM_A), 1.0),
        'cache_kidx': nrm(ks[4], (DEPTH, n_pool, PAGE_SIZE, IDX_DIM), 1.0),
        'state_wkv': nrm(ks[5], (DEPTH, DEC_BATCH, N_HEADS_B, HEAD_B, HEAD_B), 0.5),
        'state_shift': nrm(ks[6], (DEPTH, DEC_BATCH, D_MODEL), 1.0),
        'page_table': page_table,
        'g_mix': 1.0 + nrm(ks[8], (DEPTH, D_MODEL), 0.02),
        'w_in': nrm(ks[9], (DEPTH, D_MODEL, N_IN_A + N_IN_B), D_MODEL ** -0.5),
        'mu_b': jax.random.uniform(ks[10], (DEPTH, N_IN_B), f32),
        'w0': jax.random.uniform(ks[11], (DEPTH, C_B), f32, -6.0, -1.0),
        'w2': nrm(ks[12], (DEPTH, D_DECAY, C_B), D_DECAY ** -0.5),
        'a0': nrm(ks[13], (DEPTH, C_B), 0.1),
        'a2': nrm(ks[14], (DEPTH, D_AAA, C_B), D_AAA ** -0.5),
        'g2': nrm(ks[15], (DEPTH, D_GATE, C_B), D_GATE ** -0.5),
        'k_k': 0.85 + nrm(ks[16], (DEPTH, C_B), 0.02),
        'k_a': 1.0 + nrm(ks[17], (DEPTH, C_B), 0.02),
        'r_k': nrm(ks[18], (DEPTH, N_HEADS_B, HEAD_B), 0.1),
        'lnx_w': 1.0 + nrm(ks[19], (DEPTH, C_B), 0.02),
        'lnx_b': nrm(ks[20], (DEPTH, C_B), 0.01),
        'w_pa': nrm(ks[21], (DEPTH, C_A, D_MODEL), C_A ** -0.5),
        'w_pb': nrm(ks[22], (DEPTH, C_B, D_MODEL), C_B ** -0.5),
        'w_o': nrm(ks[23], (DEPTH, D_MODEL, D_MODEL), D_MODEL ** -0.5),
        'g_ffn': 1.0 + nrm(ks[24], (DEPTH, D_MODEL), 0.02),
        'w_gate': nrm(ks[25], (DEPTH, D_MODEL, D_FF), D_MODEL ** -0.5),
        'w_up': nrm(ks[26], (DEPTH, D_MODEL, D_FF), D_MODEL ** -0.5),
        'w_down': nrm(ks[27], (DEPTH, D_FF, D_MODEL), D_FF ** -0.5),
        'g_final': 1.0 + nrm(ks[28], (D_MODEL,), 0.02),
    }

def reference(x_prompt, x_sample, cache_k, cache_v, cache_kidx, state_wkv, state_shift, page_table,
              g_mix, w_in, mu_b, w0, w2, a0, a2, g2, k_k, k_a, r_k, lnx_w, lnx_b,
              w_pa, w_pb, w_o, g_ffn, w_gate, w_up, w_down, g_final):
    B = x_prompt.shape[0]
    past_len = page_table.shape[1] * PAGE_SIZE
    xp, xs = x_prompt, x_sample
    kp_l, vp_l, kip_l, wkvp_l, shp_l = [], [], [], [], []
    ks_l, vs_l, kis_l, wkvs_l, shs_l = [], [], [], [], []
    for l in range(DEPTH):
        p = {'g_mix': g_mix[l], 'w_in': w_in[l], 'mu_b': mu_b[l], 'w0': w0[l], 'w2': w2[l],
             'a0': a0[l], 'a2': a2[l], 'g2': g2[l], 'k_k': k_k[l], 'k_a': k_a[l], 'r_k': r_k[l],
             'lnx_w': lnx_w[l], 'lnx_b': lnx_b[l], 'w_pa': w_pa[l], 'w_pb': w_pb[l], 'w_o': w_o[l],
             'g_ffn': g_ffn[l], 'w_gate': w_gate[l], 'w_up': w_up[l], 'w_down': w_down[l]}
        h0 = jnp.zeros((B, D_MODEL), xp.dtype)
        s0 = jnp.zeros((B, N_HEADS_B, HEAD_B, HEAD_B), xp.dtype)
        xp, kp, vp, kip, wkvp, shp = _layer(xp, h0, s0, 0, _attn_prompt, p)
        attn_s = functools.partial(_attn_sample, cache_k=cache_k, cache_v=cache_v, cache_ki=cache_kidx,
                                   page_table=page_table, layer=l)
        xs, ksm, vsm, kism, wkvs, shs = _layer(xs, state_shift[l], state_wkv[l], past_len, attn_s, p)
        kp_l.append(kp); vp_l.append(vp); kip_l.append(kip); wkvp_l.append(wkvp); shp_l.append(shp)
        ks_l.append(ksm); vs_l.append(vsm); kis_l.append(kism); wkvs_l.append(wkvs); shs_l.append(shs)
    y_prompt = _rmsnorm(xp, g_final)
    y_sample = _rmsnorm(xs, g_final)
    k_prompt = jnp.stack(kp_l)
    v_prompt = jnp.stack(vp_l)
    kidx_prompt = jnp.stack(kip_l)
    wkv_prompt = jnp.stack(wkvp_l)
    shift_prompt = jnp.stack(shp_l)
    k_sample = jnp.stack(ks_l)
    v_sample = jnp.stack(vs_l)
    kidx_sample = jnp.stack(kis_l)
    wkv_sample = jnp.stack(wkvs_l)
    shift_sample = jnp.stack(shs_l)
    return (y_prompt, y_sample, k_prompt, v_prompt, kidx_prompt, wkv_prompt, shift_prompt,
            k_sample, v_sample, kidx_sample, wkv_sample, shift_sample)


_drawn_inputs = setup_inputs


def setup_inputs(seed=0):
    import zlib

    import numpy as np

    out = dict(_drawn_inputs(seed))
    spreads = {}
    factors = {'k_k': 8.856,
     'k_a': 2.754,
     'lnx_w': 8.0,
     'lnx_b': 36.346,
     'g_ffn': 3.938,
     'g_final': 7.455}
    for name, (base, spread) in spreads.items():
        noise = np.random.default_rng([zlib.crc32(name.encode()), seed]).standard_normal(out[name].shape)
        drawn = base * np.exp(spread * noise) if base else spread * noise
        out[name] = __import__('jax').numpy.asarray(drawn.astype(out[name].dtype))
    for name, factor in factors.items():
        out[name] = (out[name] * factor).astype(out[name].dtype)
    return out
```

```python
from contextlib import ExitStack

import numpy as np

import concourse.bass as bass
from concourse import mybir

F32 = mybir.dt.float32
I32 = mybir.dt.int32
ALU = mybir.AluOpType
ACT = mybir.ActivationFunctionType
AX = mybir.AxisListType

P = 128
DM, SEQ, NB, NS, PAST, PAGE = 2048, 256, 8, 4, 1024, 128
NSAMP = NB * NS
NT = SEQ + NSAMP
NX = NT + NB
KT = DM // P
HA, DH = 8, 128
IH, IDIM = 8, 64
HB, DB = 16, 64
CT = HB * DB // P
DFF = 5632
FT = DFF // P
FQ = FT // 4
NPG = PAST // PAGE
CH = 32
NCH = SEQ // CH
TOPK_P, TOPK_S = 64, 256
POOL = (NB * NPG) + (NB * NPG) // 4
EPS, LNX_EPS = 1e-6, 64e-5
SCALE = DH ** -0.5
WI_SCALE = IH ** -0.5 * IDIM ** -0.5
NEG, TAKEN = -1e30, -3e38
E_HALF = float(np.exp(-0.5))

U_SMALL, U_RKV, U_IDX, U_QKV, U_GA, U_MIX, U_O, U_FF = 0, 3, 27, 33, 57, 73, 105, 121
U_DOWN = U_FF + 2 * FT
U_END = U_DOWN + 4 * KT

CONST = {}
_at = 0
for _n, _w in (("ident", 128), ("ones", 128), ("blk", 128), ("ropeA", 128), ("cosA", NT), ("sinA", NT),
               ("ropeI", 128), ("cosI", NT), ("sinI", NT), ("gmask", 64), ("negtri", 512),
               ("negblk", 36), ("spread", 32), ("dmask", 32), ("oneseq", NB + 1), ("pick", NSAMP),
               ("keep", SEQ)):
    CONST[_n] = (_at, _w)
    _at += _w
NCONST = _at
PRM = {}
_at = 0
for _n, _w in (("g_mix", 16), ("g_ffn", 16), ("g_final", 16), ("mu", 27), ("w0", 8), ("a0", 8), ("k_k", 8),
               ("k_a", 8), ("r_k", 8), ("lnx_w", 8), ("lnx_b", 8)):
    PRM[_n] = (_at, _w)
    _at += _w
NPRM = _at


def constants():
    c = np.zeros((P, NCONST), np.float32)

    def put(name, a):
        at, w = CONST[name]
        c[: a.shape[0], at:at + a.shape[1]] = a

    put("ident", np.eye(P))
    put("ones", np.ones((P, P)))
    put("blk", np.kron(np.eye(2), np.ones((64, 64))))
    pos = np.concatenate([np.arange(SEQ), np.tile(PAST + np.arange(NS), NB)]).astype(np.float32)
    for name, d, reps in (("A", DH, 1), ("I", IDIM, 2)):
        rot = d // 4
        half = rot // 2
        inv = np.float32(500000.0) ** (-np.arange(half, dtype=np.float32) * np.float32(2.0) / np.float32(rot))
        ang = inv.astype(np.float32)[:, None] * pos[None, :]
        cos, sin = np.ones((d, NT), np.float32), np.zeros((d, NT), np.float32)
        cos[:half] = cos[half:rot] = np.cos(ang)
        sin[:half] = sin[half:rot] = np.sin(ang)
        r = np.zeros((d, d), np.float32)
        for j in range(half):
            r[j, j + half] = -1.0
            r[j + half, j] = 1.0
        put("rope" + name, np.kron(np.eye(reps), r).T)
        put("cos" + name, np.tile(cos, (reps, 1)))
        put("sin" + name, np.tile(sin, (reps, 1)))
    s, t = np.arange(CH)[:, None], np.arange(CH)[None, :]
    put("gmask", np.tile(np.concatenate([s < t, s <= t], 1).astype(np.float32), (4, 1)))
    q, k = np.arange(SEQ)[:, None], np.arange(SEQ)[None, :]
    put("negtri", np.where(k > q, NEG, 0.0).reshape(2, P, SEQ).transpose(1, 0, 2).reshape(P, -1))
    b, tt = np.arange(NSAMP) // NS, np.arange(NSAMP) % NS
    future = np.where(np.arange(NS)[None, :] > tt[:, None], NEG, 0.0)
    other = np.where((b[:, None] != b[None, :]) | (tt[None, :] > tt[:, None]), NEG, 0.0)
    put("negblk", np.concatenate([future, other], 1))
    put("spread", np.repeat(np.eye(IH), NS, axis=1))
    put("dmask", (tt[:, None] == tt[None, :]).astype(np.float32))
    put("oneseq", (b[:, None] == np.arange(NB)[None, :]).astype(np.float32))
    put("pick", np.tile(np.eye(NSAMP), (4, 1)))
    put("keep", np.tile((np.arange(SEQ) % CH != 0).astype(np.float32), (P, 1)))
    return c


def program(nc, wst, wdn, xT, cst_d, prm_d, lora_d, kT_d, v_d, ki_d, wkv_d, pt_d, o_y, o_k, o_v, o_ki, o_wkv,
            o_shift, o_wkvs):
    with ExitStack() as ctx:
        def sb(name, shape, dt=F32):
            return ctx.enter_context(nc.sbuf_tensor(name, shape, dt))

        sems = {}

        def sem(name):
            if name not in sems:
                sems[name] = ctx.enter_context(nc.semaphore(name))
            return sems[name]

        cst, prm = sb("cst", [P, NCONST]), sb("prm", [P, NPRM])
        ring = sb("ring", [P, 4, KT, P])
        hT = sb("hT", [P, KT, NX])
        ar = sb("arena", [P, 35520])
        ptab = sb("ptab", [1, NB * NPG], I32)
        small = sb("small", [P, 1420])

        def c_(name):
            at, w = CONST[name]
            return cst[:, at:at + w]

        def p_(name, j, n=1):
            at, w = PRM[name]
            return prm[:, at + j:at + j + n]

        def area(at, *shape):
            n = int(np.prod(shape))
            v = ar[:, at:at + n]
            if len(shape) == 2:
                v = v.rearrange("p (a b) -> p a b", b=shape[1])
            if len(shape) == 3:
                v = v.rearrange("p (a b c) -> p a b c", b=shape[1], c=shape[2])
            return v

        R, K, VP = area(0, CT, NT), area(2304, CT, NT), area(4608, CT, CH + NT)
        V = VP[:, :, CH:]
        AA, DEC, KK, BV = area(7168, CT, NT), area(9472, CT, NT), area(11776, CT, NT), area(14080, CT, NT)
        ARt, BKt = area(16384, NCH, CT, 64), area(20480, NCH, CT, 64)
        Q, KA, VA = area(24576, HA, NT), area(26880, HA, NT), area(29184, HA, NT)
        QK = area(24576, 2 * HA, NT)
        QI, KI, WI = area(31488, 4, NT), area(32640, NT), area(32928, NT)
        IDXT = area(31488, 5, NT)
        YT = area(33216, CT, NT)
        RSTD = area(33216, NT)
        XT = area(16384, KT, NT)
        SQ = area(24576, KT, NT)
        PV = area(20480 + 1024, 2, NT)
        LORA = area(20480 + 1024 + 2 * NT, 1024)
        SW = area(20480 + 2048 + 2 * NT, NT)
        DIF = area(20480 + 2048 + 3 * NT, NT)
        RK = area(0, 2 * CT, NT)
        LAST = area(16384 + 4608, KT, 1 + NB)
        ROPI, ROPT = area(0, 2, NT), area(22528, 2, NT)
        D0, D1 = area(16384, CT, SEQ), area(16384 + SEQ * CT, CT, SEQ)
        PD, PI = area(24576, CT, SEQ), area(26880, CT, SEQ)
        RW = area(29184, 2, HB * DB)
        SCP = area(0, 2, SEQ)
        SCS = area(512, PAST + NS)
        RL = area(1540, PAST + NS)
        RL2 = area(1540, 2, SEQ)
        SC4 = area(2568, PAST + NS)
        KIB = area(16384, 2, PAST)
        sm_at = [0]

        def sml(*shape):
            n = int(np.prod(shape))
            v = small[:, sm_at[0]:sm_at[0] + n]
            sm_at[0] += n
            if len(shape) == 2:
                v = v.rearrange("p (a b) -> p a b", b=shape[1])
            if len(shape) == 3:
                v = v.rearrange("p (a b c) -> p a b c", b=shape[1], c=shape[2])
            return v


        SG = sml(2, NT)
        MP = sml(2, SEQ)
        ps = [ctx.enter_context(nc.psum_tensor(f"ps{i}", [P, 512], F32)) for i in range(8)]

        rows_d = nc.dram_tensor("sample_rows", (6, NSAMP, HB * DB), F32)
        arbk_d = nc.dram_tensor("chunk_ar_bk", (2, NCH, P, CT * 64), F32)
        gram_d = nc.dram_tensor("gram", (NCH, P, CT * 64), F32)
        inv_d = nc.dram_tensor("inverse", (NCH, 2, CH, CT, CH), F32)
        sc_d = nc.dram_tensor("sample_scores", (NSAMP, PAST + NS), F32)
        yrow_d = nc.dram_tensor("sample_y", (NSAMP, HB * DB), F32)

        WR, WS = sml(2, IH), sml(NSAMP)
        QS, WSB = sml(2, NSAMP), sml(2, NS)
        M8 = sml(3, 8)
        PC = sml(CT, NCH)
        ROWMAX, ROWSUM = sml(2, 1), sml(2, 1)
        GS = area(24576, 2, CT * 64)
        GL, TI, TMP = area(18432, CH, CH), area(19456, CH, CH), area(20480, CH, CH)
        SAR, SBK = area(16384, CT, 64), area(16896, CT, 2, 64)
        SGR, STI = area(17920, CT, 64), area(18432, CT, CH)
        SV = area(18688, CT, 2, 64)
        UV, XS, BR = area(19712, CT, 64), area(20224, CT, 64), area(20736, CT, 64)
        ST = area(22528, CT, 64)
        S2, TA, TY = area(9472, 32, 64), area(11520, 32, 64), area(13568, 32, 64)
        SR = area(31488, 6, NS, 64)
        SY, SA = area(15616, NS, 64), area(15872, 32)
        YR = area(22528 + 512, HB * DB)
        GA = area(0, KT, NT)
        OA = area(4608, HA, NT)
        VR = area(2304, 2, HA * DH)
        VS = area(29184, HA * DH)
        G2 = area(9472, 2, 1024)
        YM, YD, Y2 = area(11520, CT, NT), area(13824, CT, NT), area(11520, CT, NT)
        PS_, PP = area(16384, 2, SEQ), area(16896, 2, SEQ)
        PT = area(17408, 2, 2, P)
        KP, VG = area(7168, NPG, HA * P), area(7168 + 8192, NPG, HA * P)
        QZ = area(23552, HA * 36)
        QZH = area(23552, HA, NSAMP)
        SEL, PICK = area(23840, NSAMP), area(23872, NSAMP)
        MXC, NMR, NMX = area(23904, 1), area(23905, NSAMP), area(23937, 1)
        SUMC, RCP = area(23938, 1), area(23939, 1)
        MSK0 = area(21248, 4, 2 * P + NSAMP)
        MSK = area(30208, 4, 2 * P + NSAMP)
        ER, PTS = area(31488, 2 * P + NSAMP), area(31776, 3, P)
        OR = area(32160, HA * DH)
        MIXT = area(16384, KT, NT)
        XR = area(20992, KT, NT)
        SGB, T1, T2 = area(25600, 2, NT), area(26176, 2, NT), area(26752, 2, NT)
        SQ2 = area(0, KT, NT)
        ACTT = area(7168, FT, NT)
        SIL = area(0, 2, NT)
        X1 = area(20992, KT, NT)

        block = ctx.enter_context(nc.Block())

        class Chain:

            def __init__(self, eng, name):
                self.eng, self.sem, self.n, self.off = eng, sem(name), 0, 0

            def __call__(self, ins):
                ins.then_inc(self.sem, 1)
                self.n += 1
                self.eng.wait_ge(self.sem, self.off + self.n)

            def enter(self, turn, per):
                self.n0, self.per, self.off = self.n, per, turn * per

            def leave(self, turns):
                assert self.n - self.n0 == self.per, (self.n - self.n0, self.per)
                self.n, self.off = self.n0 + self.per * turns, 0

        def settle(eng):
            eng.sem_inc(sem("settled"), 1)

        def bc(a, shape):
            return a.unsqueeze(len(a.shape)).broadcast_to(shape)

        @block.sync
        def _(sp):
            sp.dma_start(XT, xT[:, :, 0:NT]).then_inc(sem("x_in"), 16)
            sp.dma_start(cst[:, :], cst_d).then_inc(sem("const_in"), 16)
            sp.dma_start(prm[:, :], prm_d).then_inc(sem("const_in"), 16)
            sp.dma_start(hT[:, :, NT:NX], xT[:, :, NT:NX]).then_inc(sem("const_in"), 16)
            sp.dma_start(ptab[:, :], pt_d).then_inc(sem("const_in"), 16)
            sp.dma_start(LORA, lora_d[0]).then_inc(sem("lora_in"), 16)

            def unit(slot, u):
                sp.dma_start(ring[:, slot].rearrange("p k c -> p (k c)"),
                             wst[bass.ds(u, 1)].rearrange("a p n -> p (a n)")).then_inc(sem(f"w_in{slot}"), 16)

            def down_unit(slot, u):
                sp.dma_start(ring[:, slot].rearrange("p k c -> p (k c)")[:, 0:FQ * P],
                             wdn[bass.ds(u, 1)].rearrange("a p n -> p (a n)")).then_inc(sem(f"w_in{slot}"), 16)

            def units(a, b, load, shift=0):
                turns = (b - a) // 4
                if turns:
                    with sp.Fori(0, turns) as i:
                        for s in range(4):
                            sp.wait_ge(sem("unit_read"), i * 4 + (a + s - 3))
                            load((a + s) % 4, i * 4 + (a + s - shift))
                for u in range(a + 4 * turns, b):
                    sp.wait_ge(sem("unit_read"), u - 3)
                    load(u % 4, u - shift)

            for u in range(4):
                unit(u, u)
            units(4, U_GA + 12, unit)

            def k_page(b, p):
                page = sp.value_load(ptab[0:1, bass.ds(b * NPG + p, 1)], min_val=0, max_val=POOL - 1)
                sp.dma_start(KP[:, p], kT_d[bass.ds(page, 1)].rearrange("a p n -> p (a n)")).then_inc(
                    sem(f"k_in{p // 4}"), 16)

            def v_page(b, p):
                page = sp.value_load(ptab[0:1, bass.ds(b * NPG + p, 1)], min_val=0, max_val=POOL - 1)
                sp.dma_start(VG[:, p], v_d[bass.ds(page, 1)].rearrange("a p n -> p (a n)")).then_inc(
                    sem(f"v_in{p // 4}"), 16)

            sp.wait_ge(sem("ob_done"), 1)
            for p in range(NPG):
                k_page(0, p)
            sp.wait_ge(sem("oa_prompt"), 2 * HA)
            sp.wait_ge(sem("wkv_out"), 16)
            for p in range(NPG):
                v_page(0, p)
            with sp.Fori(0, NB - 1) as b:
                sp.wait_ge(sem("ss_done"), b + 1)
                settle(sp)
                for p in range(NPG):
                    k_page(b + 1, p)
                sp.wait_ge(sem("pv_done"), b + 1)
                settle(sp)
                for p in range(NPG):
                    v_page(b + 1, p)
            units(U_GA + 20, U_DOWN, unit)
            units(U_DOWN, U_END, down_unit, U_DOWN)
            sp.wait_ge(sem("y_done"), 1)
            sp.dma_start(o_y, SQ2).then_inc(sem("y_out"), 16)
            sp.wait_ge(sem("y_out"), 16)
            for name, n in (("shift_out", 1), ("v_out", 1), ("k_out", 1), ("ki_out", 1), ("wkv_out", 1),
                            ("wkvs_out", 2)):
                sp.wait_ge(sem(name), 16 * n)

        @block.tensor
        def _(pe):
            mm, tr = nc.tensor.matmul, nc.tensor.transpose
            ident, ones, blk = c_("ident"), c_("ones"), c_("blk")

            def arrived(u0, s, i):
                pe.wait_ge(sem(f"w_in{(u0 + s) % 4}"), i * 16 + 16 * ((u0 + s) // 4 + 1))

            def tile(u0, s, i, rhs, n, k0=0, k1=KT):
                u = i * 4 + (u0 + s)
                if k0 == 0:
                    arrived(u0, s, i)
                    pe.wait_ge(sem("bank_free"), u + 1)
                slot, out = (u0 + s) % 4, ps[(u0 + s) % 2][:, 0:n]
                for k in range(k0, k1):
                    ins = mm(out, ring[:, slot, k, :], rhs(k), start=(k == 0), stop=(k == KT - 1))
                if k1 == KT:
                    ins.then_inc(sem("unit_read"), 1)

            def tiles(u0, u1, rhs, n):
                pe.wait_ge(sem("bank_free"), u0 + 2)
                turns = (u1 - u0) // 4
                if turns > 1:
                    with pe.Fori(0, turns) as i:
                        for s in range(4):
                            tile(u0, s, i, rhs, n)
                else:
                    turns = 0
                for u in range(u0 + 4 * turns, u1):
                    tile(u, 0, 0, rhs, n)

            h_all, h_tok = (lambda k: hT[:, k, :]), (lambda k: hT[:, k, 0:NT])

            def total_squares(n, src):
                for k in range(KT):
                    if k % 4 == 0:
                        pe.wait_ge(sem("squares"), 4 * n + k // 4 + 1)
                    ins = mm(ps[7][:, 0:NT], ones, src[:, k, :], start=(k == 0), stop=(k == KT - 1))
                ins.then_inc(sem("squares_summed"), 1)

            pe.sem_inc(sem("bank_free"), 2)
            pe.sem_inc(sem("chunk_done"), 1)
            pe.wait_ge(sem("const_in"), 64)
            total_squares(0, SQ)
            pe.wait_ge(sem("h_done"), 1)
            tiles(0, 3, h_all, NX)
            tiles(U_RKV, U_IDX, h_all, NX)

            pe.wait_ge(sem("lora_in"), 16)
            pe.wait_ge(sem("sw_done"), 1)
            for j in range(2 * CT):
                if j >= 4:
                    pe.wait_ge(sem("lora_out"), j - 3)
                at = 64 * (j // CT)
                mm(ps[2 + j % 4][:, 0:NT], LORA[at:at + 64, (j % CT) * P:(j % CT + 1) * P], SW[at:at + 64, :],
                   start=True, stop=True).then_inc(sem("lora"), 1)
            pe.wait_ge(sem("kk_sq"), 1)
            for j in range(CT):
                pe.wait_ge(sem("lora_out"), min(16, 13 + j))
                if j >= 4:
                    pe.wait_ge(sem("norm_out"), j - 3)
                mm(ps[2 + j % 4][:, 0:NT], blk, BV[:, j, :], start=True, stop=True).then_inc(sem("norm"), 1)
            tiles(U_IDX, U_QKV, h_tok, NT)
            pe.wait_ge(sem("rk_done"), 1)
            pe.wait_ge(sem("norm_out"), CT)
            for j in range(CT):
                if j >= 4:
                    pe.wait_ge(sem("bonus_out"), j - 3)
                mm(ps[2 + j % 4][:, 0:NT], blk, AA[:, j, :], start=True, stop=True).then_inc(sem("bonus"), 1)
            pe.wait_ge(sem("bonus_out"), CT)
            pe.wait_ge(sem("dec_done"), 1)
            for a, src in enumerate((R, DEC, K, V, KK, BV)):
                if a >= 2:
                    pe.wait_ge(sem("rows_out"), 2 * (a - 1))
                for j in range(CT):
                    ins = tr(ps[2 + 2 * (a % 2) + j // 4][0:NSAMP, (j % 4) * P:(j % 4 + 1) * P],
                             src[:, j, SEQ:NT], ident)
                ins.then_inc(sem("rows"), 1)
            pe.wait_ge(sem("bank_free"), U_QKV + 2)
            for j in range(5):
                if j >= 2:
                    pe.wait_ge(sem("rope_idx_out"), j - 1)
                mm(ps[6 + j % 2][:, 0:NT], c_("ropeI"), IDXT[:, j, :], start=True, stop=True).then_inc(
                    sem("rope_idx"), 1)
            pe.wait_ge(sem("rope_idx_out"), 5)
            for qt in range(2):
                tr(ps[6][:, qt * IH:(qt + 1) * IH], WI[0:IH, qt * P:(qt + 1) * P], ident[0:IH, 0:IH])
            mm(ps[6][0:NSAMP, 64:64 + NSAMP], c_("spread")[0:IH, :], WI[0:IH, SEQ:NT], start=True,
               stop=True).then_inc(sem("wi"), 1)
            pe.wait_ge(sem("arbk_done"), 1)
            pe.wait_ge(sem("rows_out"), 12)
            for c in range(NCH):
                if c >= 2:
                    pe.wait_ge(sem("gram_out"), c - 1)
                for h in range(HB):
                    at, j = 64 * (h % 2), h // 2
                    ins = mm(ps[2 + c % 2][at:at + 64, j * 64:(j + 1) * 64],
                             BKt[at:at + 64, c, j, :], ARt[at:at + 64, c, j, :], start=True, stop=True)
                ins.then_inc(sem("gram"), 1)
            pe.wait_ge(sem("gram_out"), NCH)
            pe.wait_ge(sem("wi_out"), 1)
            for n in range(2 * IH):
                qt, h = n // IH, n % IH
                if n >= 4:
                    pe.wait_ge(sem("pidx_relu"), n - 3)
                at = 64 * (h % 2)
                mm(ps[2 + n % 4][:, 0:SEQ], QI[at:at + 64, h // 2, qt * P:(qt + 1) * P], KI[at:at + 64, 0:SEQ],
                   start=True, stop=True).then_inc(sem("pidx"), 1)
            pe.wait_ge(sem("pidx_relu"), 2 * IH)
            with pe.Fori(0, NB // 2) as i:
                for s in range(2):
                    pe.wait_ge(sem(f"ki_in{s}"), i * (16 * NPG) + 16 * NPG)
                    pe.wait_ge(sem("qs_done"), i * 2 + (s + 1))
                    pe.wait_ge(sem("sidx_relu"), i * 6 + 3 * (s + 1))
                    for half in range(2):
                        mm(ps[2 + half][0:NSAMP, :], QS[:, s, :], KIB[:, s, half * 512:(half + 1) * 512],
                           start=True, stop=True)
                    mm(ps[4][0:NSAMP, 0:NS], QS[:, s, :], KI[:, bass.ds(i * 2 * NS + (SEQ + s * NS), NS)],
                       start=True, stop=True).then_inc(sem("sidx"), 1)
                    pe.wait_ge(sem("sidx_relu"), i * 6 + 3 * (s + 2))
                    pe.wait_ge(sem("sc_out"), i * 2 + (s + 1))
                    settle(pe)
                    for half in range(2):
                        mm(ps[5 + half][0:NS, :], WSB[0:NSAMP, s, :], RL[0:NSAMP, half * 512:(half + 1) * 512],
                           start=True, stop=True)
                    mm(ps[7][0:NS, 0:NS], WSB[0:NSAMP, s, :], RL[0:NSAMP, PAST:PAST + NS],
                       start=True, stop=True).then_inc(sem("sidx_sum"), 1)

            tiles(U_QKV, U_GA, h_tok, NT)
            pe.wait_ge(sem("bank_free"), U_GA + 2)
            pe.wait_ge(sem("sc_out"), NB + 1)
            with pe.Fori(0, HA) as i:
                for s in range(2):
                    pe.wait_ge(sem("rope_out"), i * 2 + (s + 1))
                    mm(ps[6 + s][:, 0:NT], c_("ropeA"), QK[:, bass.ds(i * 2 + s, 1), :].rearrange("p a n -> p (a n)"),
                       start=True, stop=True).then_inc(sem("rope"), 1)
            pe.wait_ge(sem("rope_out"), 2 + 2 * HA)

            def chunk(i, s):
                n = i * 4 + s
                tile(U_GA, s, i, h_tok, NT)
                pe.wait_ge(sem("sbk_in"), i * 128 + 32 * (s + 1))
                pe.wait_ge(sem("sv_done"), 2 * n + 2)
                settle(pe)
                for j in range(CT):
                    tr(ps[4 + j // 4][:, (j % 4) * P:(j % 4 + 1) * P], SBK[:, j].rearrange("p a n -> p (a n)"), ident)
                for j in range(CT):
                    ins = tr(ps[2 + j // 4][:, (j % 4) * P:(j % 4 + 1) * P], SV[:, j].rearrange("p a n -> p (a n)"),
                             ident)
                ins.then_inc(sem("turned"), 1)
                pe.wait_ge(sem("sgr_in"), i * 64 + 16 * (s + 1))
                pe.wait_ge(sem("sar_in"), i * 64 + 16 * (s + 1))
                pe.wait_ge(sem("turned_out"), 4 * n + 4)
                pe.wait_ge(sem("state"), n + 1)
                settle(pe)
                for h in range(HB):
                    at, j = 64 * (h % 2), h // 2
                    out = ps[2][at:at + CH, j * 64:(j + 1) * 64]
                    mm(out, SAR[at:at + 64, j, 0:CH], ST[at:at + 64, j, :], start=True, stop=False)
                    ins = mm(out, SGR[at + CH:at + 64, j, 0:CH], UV[at + CH:at + 64, j, :], start=False, stop=True,
                             tile_position=(at + CH, at))
                ins.then_inc(sem("x_done"), 1)
                pe.wait_ge(sem("sti_in"), i * 128 + 32 * (s + 1))
                pe.wait_ge(sem("x_out"), 2 * n + 2)
                pe.wait_ge(sem("br_out"), 4 * n + 4)
                settle(pe)
                for h in range(HB):
                    at, j = 64 * (h % 2), h // 2
                    ins = mm(ps[4][at:at + CH, j * 64:(j + 1) * 64], STI[at:at + CH, j, :], XS[at:at + CH, j, :],
                             start=True, stop=True)
                ins.then_inc(sem("u_done"), 1)
                pe.wait_ge(sem("u_out"), 2 * n + 2)
                pe.wait_ge(sem("y_out_of_bank"), n + 1)
                settle(pe)
                for h in range(HB):
                    at, j = 64 * (h % 2), h // 2
                    mm(ps[6][at:at + 64, j * CH:(j + 1) * CH], ST[at:at + 64, j, :], SAR[at:at + 64, j, CH:64],
                       start=True, stop=False)
                    mm(ps[6][at:at + 64, j * CH:(j + 1) * CH], UV[at:at + 64, j, :], SGR[at:at + 64, j, CH:64],
                       start=False, stop=True)
                for h in range(HB):
                    at, j = 64 * (h % 2), h // 2
                    ins = mm(ps[7][at:at + 64, j * 64:(j + 1) * 64], BR[at:at + 64, j, :], UV[at:at + 64, j, :],
                             start=True, stop=True)
                ins.then_inc(sem("chunk_done"), 1)

            with pe.Fori(0, 2) as i:
                for s in range(4):
                    chunk(i, s)

            pe.wait_ge(sem("yrow_in"), 16)
            pe.wait_ge(sem("state"), NCH + 1)
            pe.wait_ge(sem("y_out_of_bank"), NCH + 1)
            for j in range(CT):
                ins = tr(ps[2][:, j * NSAMP:(j + 1) * NSAMP], YR[0:NSAMP, j * P:(j + 1) * P], ident[0:NSAMP, 0:NSAMP])
            ins.then_inc(sem("yT"), 1)
            pe.wait_ge(sem("yT_out"), 1)
            for j in range(CT):
                if j >= 4:
                    pe.wait_ge(sem("mean_out"), j - 3)
                mm(ps[3 + j % 4][:, 0:NT], blk, YT[:, j, :], start=True, stop=True).then_inc(sem("mean"), 1)
            pe.wait_ge(sem("g2_in"), 32)
            for j in range(CT):
                pe.wait_ge(sem("mean_out"), min(CT, 5 + j))
                if j >= 4:
                    pe.wait_ge(sem("gate_out"), j - 3)
                out = ps[3 + j % 4][:, 0:NT]
                mm(out, G2[:, 0, j * P:(j + 1) * P], SG[:, 0, :], start=True, stop=False)
                mm(out, G2[0:32, 1, j * P:(j + 1) * P], SG[0:32, 1, :], start=False, stop=True).then_inc(
                    sem("gate"), 1)
            pe.wait_ge(sem("y_sq"), 1)
            for j in range(CT):
                pe.wait_ge(sem("gate_out"), min(CT, 5 + j))
                if j >= 4:
                    pe.wait_ge(sem("var_out"), j - 3)
                mm(ps[3 + j % 4][:, 0:NT], blk, Y2[:, j, :], start=True, stop=True).then_inc(sem("var"), 1)

            pe.wait_ge(sem("var_out"), CT)
            for t in range(2):
                for h in range(HA):
                    ins = tr(ps[2 + 2 * t + h // 4][:, (h % 4) * P:(h % 4 + 1) * P], VA[:, h, t * P:(t + 1) * P], ident)
            for h in range(HA):
                ins = tr(ps[6 + h // 4][0:NSAMP, (h % 4) * P:(h % 4 + 1) * P], VA[:, h, SEQ:NT], ident)
            ins.then_inc(sem("vrows"), 1)
            pe.wait_ge(sem("vrows_out"), 6)

            def pscore(n):
                qt, h = n // HA, n % HA
                if n >= 2:
                    pe.wait_ge(sem("ps_out"), n - 1)
                mm(ps[2 + n % 2][:, 0:SEQ], Q[:, h, qt * P:(qt + 1) * P], KA[:, h, 0:SEQ],
                   start=True, stop=True).then_inc(sem("ps_done"), 1)

            def pturn(n):
                pe.wait_ge(sem("pp_done"), n + 1)
                if n >= 2:
                    pe.wait_ge(sem("pt_out"), n - 1)
                for k in range(2):
                    ins = tr(ps[4 + n % 2][:, k * P:(k + 1) * P], PP[:, n % 2, k * P:(k + 1) * P], ident)
                ins.then_inc(sem("pt_done"), 1)

            def pvalue(n):
                qt, h = n // HA, n % HA
                pe.wait_ge(sem("pt_out"), n + 1)
                if n >= 2:
                    pe.wait_ge(sem("oa_prompt"), n - 1)
                for k in range(2):
                    ins = mm(ps[6 + n % 2][:, 0:P], VR[:, k, h * P:(h + 1) * P], PT[:, n % 2, k, :],
                             start=(k == 0), stop=(k == 1))
                ins.then_inc(sem("pv_prompt"), 1)

            for n in range(2 * HA + 2):
                if n < 2 * HA:
                    pscore(n)
                if 1 <= n <= 2 * HA:
                    pturn(n - 1)
                if n >= 2:
                    pvalue(n - 2)

            pe.wait_ge(sem("oa_prompt"), 2 * HA)

            def sequence(i, s):
                n = i * 4 + s
                pe.wait_ge(sem("qb_done"), n + 1)
                pe.wait_ge(sem("sel_done"), n + 1)
                pe.wait_ge(sem("ex_done"), n + 1)
                for a in range(2):
                    pe.wait_ge(sem(f"k_in{a}"), i * 256 + 64 * (s + 1))
                settle(pe)
                for j in range(4):
                    mm(ps[2][32 * j:32 * j + 32, 0:2 * P + NSAMP], SEL[0:NSAMP, :], MSK[0:NSAMP, j, :],
                       start=True, stop=False, skip_group_check=True)
                for h in range(HA):
                    mm(ps[2][0:32, 2 * P:2 * P + NSAMP], QZH[:, h, :], KA[:, h, SEQ:NT], start=False, stop=(h == HA - 1),
                       skip_group_check=True)
                for h in range(HA):
                    for j in range(4):
                        ins = mm(ps[2][32 * j:32 * j + 32, 0:2 * P], QZH[:, h, :],
                                 KP[:, 2 * j:2 * j + 2, h * P:(h + 1) * P], start=False, stop=(h == HA - 1),
                                 skip_group_check=True)
                ins.then_inc(sem("ss_done"), 1)
                tile(U_GA + 8, s, i, h_tok, NT, 0, 4)
                pe.wait_ge(sem("mx_done"), n + 1)
                tr(ps[3][0:1, 0:P], MXC, ident).then_inc(sem("mxT"), 1)
                tile(U_GA + 8, s, i, h_tok, NT, 4, 7)
                pe.wait_ge(sem("nm_done"), n + 1)
                settle(pe)
                for j in range(4):
                    ins = mm(ps[3][32 * j:32 * j + 32, P:P + 1], NMR[0:1, :], ones[0:1, 0:1], start=True, stop=True)
                ins.then_inc(sem("mb"), 1)
                tile(U_GA + 8, s, i, h_tok, NT, 7, 12)
                pe.wait_ge(sem("ex_done"), n + 2)
                for half in range(2):
                    tr(ps[4][:, half * P:(half + 1) * P], ER[:, half * P:(half + 1) * P], ident)
                tr(ps[4][0:NSAMP, 2 * P:2 * P + NSAMP], ER[0:NSAMP, 2 * P:], ident[0:NSAMP, 0:NSAMP]).then_inc(
                    sem("et_done"), 1)
                for j in range(4):
                    ins = mm(ps[3][32 * j:32 * j + 32, P + 1:P + 2], c_("pick"), SUMC, start=True, stop=True)
                ins.then_inc(sem("den"), 1)
                tile(U_GA + 8, s, i, h_tok, NT, 12, KT)
                pe.wait_ge(sem("pts_done"), n + 1)
                for c in range(2):
                    pe.wait_ge(sem(f"v_in{c}"), i * 256 + 64 * (s + 1))
                for half in range(2):
                    for c in range(2):
                        for j in range(4):
                            mm(ps[5 + c][32 * j:32 * j + 32, :], PTS[:, half, 32 * j:32 * j + 32],
                               VG[:, 2 * j + half, c * 512:(c + 1) * 512], start=(half == 0),
                               stop=(half == 1 and j > 0), skip_group_check=True)
                for c in range(2):
                    ins = mm(ps[5 + c][0:32, :], PTS[0:NSAMP, 2, 0:NSAMP], VS[0:NSAMP, c * 512:(c + 1) * 512],
                             start=False, stop=True, skip_group_check=True)
                ins.then_inc(sem("pv_done"), 1)
                pe.wait_ge(sem("pick_done"), n + 1)
                pe.wait_ge(sem("or_done"), i * 8 + 2 * (s + 1))
                pe.wait_ge(sem("oa_out"), n + 1)
                for h in range(HA):
                    ins = mm(ps[7][:, h * NS:(h + 1) * NS], OR[:, h * P:(h + 1) * P],
                             PICK[:, h * NS:(h + 1) * NS], start=True, stop=True)
                ins.then_inc(sem("os_done"), 1)

            with pe.Fori(0, 2) as i:
                for s in range(4):
                    sequence(i, s)

            pe.wait_ge(sem("oa_out"), NB + 1)
            pe.wait_ge(sem("bank_free"), U_MIX + 2)
            with pe.Fori(0, KT // 2) as i:
                for s in range(2):
                    u0 = U_MIX + 2 * s
                    pe.wait_ge(sem("mix_free"), i * 2 + (s + 1))
                    arrived(u0, 0, i)
                    for k in range(KT):
                        ins = mm(ps[3 * s][:, 0:NT], ring[:, u0 % 4, k, :], hT[:, k, 0:NT],
                                 start=(k == 0), stop=(k == KT - 1))
                    ins.then_inc(sem("unit_read"), 1)
                    arrived(u0, 1, i)
                    for part, src in enumerate((OA, YT)):
                        for k in range(CT):
                            ins = mm(ps[3 * s + 1 + part][:, 0:NT], ring[:, (u0 + 1) % 4, part * CT + k, :],
                                     src[:, k, :], start=(k == 0), stop=(k == CT - 1))
                    ins.then_inc(sem("unit_read"), 1)
            pe.wait_ge(sem("mix_free"), KT + 2)

            with pe.Fori(0, KT // 4) as i:
                for s in range(4):
                    arrived(U_O, s, i)
                    pe.wait_ge(sem("o_free"), i * 4 + (s + 1))
                    for k in range(KT):
                        ins = mm(ps[s % 2][:, 0:NT], ring[:, (U_O + s) % 4, k, :], MIXT[:, k, :],
                                 start=(k == 0), stop=(k == KT - 1))
                    ins.then_inc(sem("unit_read"), 1)
            total_squares(1, SQ2)
            pe.wait_ge(sem("h_done"), 2)
            with pe.Fori(0, FT // 2) as i:
                for s in range(4):
                    arrived(U_FF, s, i)
                    if s % 2 == 0:
                        pe.wait_ge(sem("ff_free"), i * 2 + (s // 2 + 1))
                    for k in range(KT):
                        ins = mm(ps[s][:, 0:NT], ring[:, (U_FF + s) % 4, k, :], hT[:, k, 0:NT],
                                 start=(k == 0), stop=(k == KT - 1))
                    ins.then_inc(sem("unit_read"), 1)
            pe.wait_ge(sem("ff_free"), FT + 2)
            with pe.Fori(0, KT // 2) as i:
                for t in range(2):
                    pe.wait_ge(sem("down_free"), i * 2 + (t + 1))
                    for q in range(4):
                        u0 = U_DOWN + 4 * t + q
                        pe.wait_ge(sem(f"w_in{u0 % 4}"), i * 32 + 16 * (u0 // 4 + 1))
                        for k in range(FQ):
                            ins = mm(ps[t][:, 0:NT], ring[:, u0 % 4, :, :].rearrange("p k c -> p (k c)")[
                                :, k * P:(k + 1) * P], ACTT[:, q * FQ + k, :], start=(q == 0 and k == 0),
                                stop=(q == 3 and k == FQ - 1))
                        ins.then_inc(sem("unit_read"), 1)
            total_squares(2, SQ2)

        @block.scalar
        def _(act):
            fn = nc.scalar.activation
            ch = Chain(act, "act_chain")

            def squares(src, dst):
                for q in range(4):
                    fn(dst[:, 4 * q:4 * q + 4, :], src[:, 4 * q:4 * q + 4, :], ACT.Square).then_inc(sem("squares"), 1)

            act.wait_ge(sem("x_in"), 16)
            squares(XT, SQ)
            act.wait_ge(sem("mean_sq"), 1)
            fn(RSTD, RSTD, ACT.Sqrt).then_inc(sem("root"), 1)

            def previous(u, par):
                act.wait_ge(sem("unit_read"), u + 1)
                act.wait_ge(sem("bank_free"), u + 1)
                bank, pv = ps[par], PV[:, par, :]
                now = bank[:, SEQ:NT].rearrange("p (b t) -> p b t", t=NS)
                out = pv[:, SEQ:NT].rearrange("p (b t) -> p b t", t=NS)
                fn(pv[:, 1:SEQ], bank[:, 0:SEQ - 1], ACT.Copy).then_inc(sem("previous"), 1)
                fn(out[:, :, 1:NS], now[:, :, 0:NS - 1], ACT.Copy).then_inc(sem("previous"), 1)
                fn(out[:, :, 0:1], bank[:, NT:NX].rearrange("p (b t) -> p b t", t=1), ACT.Copy).then_inc(
                    sem("previous"), 1)

            for u in range(3):
                previous(u, u % 2)
            act.wait_ge(sem("bank_free"), 2 + 3)
            fn(SW[0:64, :], SW[0:64, :], ACT.Tanh).then_inc(sem("sw_done"), 1)
            ch(fn(SG, SG, ACT.Sigmoid))
            with act.Fori(0, 6) as i:
                for s in range(4):
                    previous(i * 4 + (U_RKV + s), (U_RKV + s) % 2)

            for j in range(2 * CT):
                act.wait_ge(sem("lora"), j + 1)
                dst, bias = (DEC[:, j, :], p_("w0", j)) if j < CT else (AA[:, j - CT, :], p_("a0", j - CT))
                fn(dst, ps[2 + j % 4][:, 0:NT], ACT.Sigmoid, bias=bias).then_inc(sem("lora_out"), 1)
            act.wait_ge(sem("lora_out"), 2 * CT)
            fn(DEC, DEC, ACT.Exp, scale=-E_HALF).then_inc(sem("dec_done"), 1)
            act.wait_ge(sem("norm_out"), CT)
            fn(BV, BV, ACT.Sqrt).then_inc(sem("kk_root"), 1)
            for j in range(6):
                u = U_IDX + j
                act.wait_ge(sem("unit_read"), u + 1)
                dst = QI[:, j, :] if j < 4 else (KI if j == 4 else WI)
                fn(dst, ps[u % 2][:, 0:NT], ACT.Copy).then_inc(sem("bank_free"), 1)
            for a in range(6):
                act.wait_ge(sem("rows"), a + 1)
                if a >= 2:
                    act.wait_ge(sem(f"rows_stored{a % 2}"), 16 * (a // 2))
                for half in range(2):
                    fn(RW[0:NSAMP, a % 2, half * 512:(half + 1) * 512], ps[2 + 2 * (a % 2) + half][0:NSAMP, :],
                       ACT.Copy).then_inc(sem("rows_out"), 1)
            for n in range(2 * IH):
                act.wait_ge(sem("pidx"), n + 1)
                if n >= 2:
                    act.wait_ge(sem("pidx_sum"), n - 1)
                fn(RL2[:, n % 2, :], ps[2 + n % 4][:, 0:SEQ], ACT.Relu).then_inc(sem("pidx_relu"), 1)
            act.wait_ge(sem("pidx_sum"), 2 * IH)
            act.wait_ge(sem("wi_out"), 1)
            act.sem_inc(sem("sidx_relu"), 3)
            with act.Fori(0, NB // 2) as i:
                ch.enter(i, 4)
                for s in range(2):
                    b = i * 2 + s
                    q = QS[:, s, :].rearrange("p (j a t) -> p j a t", a=2, t=NS)
                    for a in range(2):
                        ch(fn(q[64 * a:64 * a + 64, :, a, :],
                              QI[64 * a:64 * a + 64, :, bass.ds(i * 2 * NS + (SEQ + s * NS), NS)], ACT.Copy))
                    fn(WSB[0:NSAMP, s, :], WS[0:NSAMP, bass.ds(i * 2 * NS + s * NS, NS)], ACT.Copy).then_inc(
                        sem("qs_done"), 1)
                    act.wait_ge(sem("sidx"), b + 1)
                    for half in range(2):
                        fn(RL[0:NSAMP, half * 512:(half + 1) * 512], ps[2 + half][0:NSAMP, :], ACT.Relu).then_inc(
                            sem("sidx_relu"), 1)
                    fn(RL[0:NSAMP, PAST:PAST + NS], ps[4][0:NSAMP, 0:NS], ACT.Relu).then_inc(sem("sidx_relu"), 1)
            ch.leave(NB // 2)

            act.wait_ge(sem("arbk_done"), 1)
            for par in range(2):
                act.wait_ge(sem(f"rows_stored{par}"), 16 * 3)
                act.wait_ge(sem(f"gram_stored{par}"), 16 * NCH // 2)
            act.wait_ge(sem("arbk_stored"), 32)
            qkv = area(24576, 3 * HA, NT)
            with act.Fori(0, 6) as i:
                for s in range(4):
                    act.wait_ge(sem("unit_read"), i * 4 + (U_QKV + s + 1))
                    fn(qkv[:, bass.ds(i * 4 + s, 1), :].rearrange("p a n -> p (a n)"), ps[(U_QKV + s) % 2][:, 0:NT],
                       ACT.Copy).then_inc(sem("bank_free"), 1)
            act.wait_ge(sem("bank_free"), U_GA + 2)
            act.dma_start(o_v, VA).then_inc(sem("v_out"), 16)
            act.wait_ge(sem("rope_out"), 2 + 2 * HA)
            act.dma_start(o_k, KA).then_inc(sem("k_out"), 16)

            act.wait_ge(sem("inv_stored"), 32 * NCH)
            act.wait_ge(sem("mask_done"), 1)

            def chunk(i, s):
                n = i * 4 + s
                act.wait_ge(sem("chunk_done"), n + 1)
                for a in range(2):
                    act.dma_start(SBK[:, :, a, :], arbk_d[1][bass.ds(n, 1)].rearrange(
                        "a p (j n) -> p (a j) n", n=64)).then_inc(sem("sbk_in"), 16)
                act.dma_start(SAR.rearrange("p a b -> p (a b)"),
                              arbk_d[0][bass.ds(n, 1)].rearrange("a p n -> p (a n)")).then_inc(sem("sar_in"), 16)
                act.dma_start(SGR.rearrange("p a b -> p (a b)"),
                              gram_d[bass.ds(n, 1)].rearrange("a p n -> p (a n)")).then_inc(sem("sgr_in"), 16)
                for a in range(2):
                    act.dma_start(STI[64 * a:64 * a + CH].rearrange("p a b -> p (a b)"),
                                  inv_d[bass.ds(n, 1), a].rearrange("a s j t -> s (a j t)")).then_inc(
                        sem("sti_in"), 16)
                for a in range(2):
                    fn(SV[:, :, a, :], VP[:, :, bass.ds(i * 4 * CH + s * CH, 2 * CH)], ACT.Copy).then_inc(
                        sem("sv_done"), 1)
                act.wait_ge(sem("unit_read"), n + (U_GA + 1))
                fn(GA[:, bass.ds(n, 1), :].rearrange("p a n -> p (a n)"), ps[(U_GA + s) % 2][:, 0:NT],
                   ACT.Copy).then_inc(sem("bank_free"), 1)
                act.wait_ge(sem("turned"), n + 1)
                for q in range(4):
                    a, half = q % 2, q // 2
                    fn(UV[64 * a + CH:64 * a + 64, half * 4:half * 4 + 4, :],
                       ps[2 + half][64 * a + CH:64 * a + 64, :].rearrange("p (j a c) -> p j a c", a=2, c=64)[:, :, a, :],
                       ACT.Copy).then_inc(sem("turned_out"), 1)
                act.wait_ge(sem("x_done"), n + 1)
                fn(XS[0:CH], ps[2][0:CH, :].rearrange("p (h i) -> p h i", i=64), ACT.Copy).then_inc(sem("x_out"), 1)
                act.wait_ge(sem("u_done"), n + 1)
                fn(UV[0:CH], ps[4][0:CH, :].rearrange("p (h i) -> p h i", i=64), ACT.Copy).then_inc(sem("u_out"), 1)
                act.wait_ge(sem("chunk_done"), n + 2)
                fn(YT[:, :, bass.ds(i * 4 * CH + s * CH, CH)],
                   ps[6][:, 0:CT * CH].rearrange("p (j t) -> p j t", t=CH), ACT.Copy).then_inc(
                    sem("y_out_of_bank"), 1)

            act.sem_inc(sem("y_out_of_bank"), 1)
            with act.Fori(0, 2) as i:
                for s in range(4):
                    chunk(i, s)
            act.wait_ge(sem("var_out"), CT)
            fn(Y2, Y2, ACT.Sqrt).then_inc(sem("var_root"), 1)

            act.wait_ge(sem("vrows"), 1)
            for t in range(2):
                for half in range(2):
                    fn(VR[:, t, half * 512:(half + 1) * 512], ps[2 + 2 * t + half][:, :], ACT.Copy).then_inc(
                        sem("vrows_out"), 1)
            act.wait_ge(sem("v_out"), 16)
            for half in range(2):
                fn(VS[0:NSAMP, half * 512:(half + 1) * 512], ps[6 + half][0:NSAMP, :], ACT.Copy).then_inc(
                    sem("vrows_out"), 1)
            for n in range(2 * HA + 1):
                if n < 2 * HA:
                    act.wait_ge(sem("nmax"), n + 1)
                    fn(PS_[:, n % 2, :], PS_[:, n % 2, :], ACT.Exp, bias=ROWMAX[:, n % 2, :],
                       accum_out=ROWSUM[:, n % 2, :]).then_inc(sem("pexp"), 1)
                if n >= 1:
                    m = n - 1
                    act.wait_ge(sem("pt_done"), m + 1)
                    if m >= 2:
                        act.wait_ge(sem("pv_prompt"), m - 1)
                    fn(PT[:, m % 2, :, :], ps[4 + m % 2][:, 0:2 * P].rearrange("p (k q) -> p k q", q=P),
                       ACT.Copy).then_inc(sem("pt_out"), 1)

            def sequence(i, s):
                n = i * 4 + s
                act.wait_ge(sem("ss_done"), n + 1)
                if s < 3:
                    nxt = i * 4 * NS + (SEQ + (s + 1) * NS)
                else:
                    nxt = -(i * 4 * NS) + (SEQ + 4 * NS)
                fn(QZD, Q[:, :, bass.ds(nxt, NS)], ACT.Copy, scale=SCALE).then_inc(sem("qb_done"), 1)
                act.wait_ge(sem("nmx_done"), n + 1)
                fn(ER, ps[2][:, 0:2 * P + NSAMP], ACT.Exp, bias=NMX, accum_out=SUMC).then_inc(sem("ex_done"), 1)
                act.wait_ge(sem("unit_read"), n + (U_GA + 9))
                fn(GA[:, bass.ds(n + 8, 1), :].rearrange("p a n -> p (a n)"), ps[(U_GA + s) % 2][:, 0:NT],
                   ACT.Copy).then_inc(sem("bank_free"), 1)
                slot = (U_GA + 12 + s) % 4
                act.dma_start(ring[:, slot].rearrange("p k c -> p (k c)"),
                              wst[bass.ds(i * 4 + (U_GA + 12 + s), 1)].rearrange("a p n -> p (a n)")).then_inc(
                    sem(f"w_in{slot}"), 16)
                act.wait_ge(sem("pv_done"), n + 1)
                fn(OR[:, 512:], ps[6][:, :], ACT.Copy).then_inc(sem("or_done"), 1)

            act.wait_ge(sem("oa_prompt"), 2 * HA)
            act.wait_ge(sem("qz_zero"), 1)
            act.sem_inc(sem("ex_done"), 1)
            QZD = QZ.rearrange("p (h x) -> p h x", x=36)[:, :, 0:NS]
            fn(QZD, Q[:, :, SEQ:SEQ + NS], ACT.Copy, scale=SCALE).then_inc(sem("qb_done"), 1)
            with act.Fori(0, 2) as i:
                for s in range(4):
                    sequence(i, s)

            act.wait_ge(sem("qb_done"), NB + 1)
            with act.Fori(0, KT // 2) as i:
                for s in range(2):
                    act.wait_ge(sem("mix_free"), i * 2 + (s + 1))
                    fn(T1[:, s, :], GA[:, bass.ds(i * 2 + s, 1), :].rearrange("p a n -> p (a n)"),
                       ACT.Sigmoid).then_inc(sem("gates"), 1)
                    act.wait_ge(sem("unit_read"), i * 4 + (U_MIX + 2 * s + 1))
                    fn(SGB[:, s, :], ps[3 * s][:, 0:NT], ACT.Sigmoid).then_inc(sem("gates"), 1)

            act.wait_ge(sem("o_free"), 2 + KT)
            squares(X1, SQ2)
            act.wait_ge(sem("mean_sq"), 2)
            fn(RSTD, RSTD, ACT.Sqrt).then_inc(sem("root"), 1)
            act.wait_ge(sem("h_done"), 2)
            with act.Fori(0, FT // 2) as i:
                for t in range(2):
                    act.wait_ge(sem("ff_free"), i * 2 + (t + 1))
                    act.wait_ge(sem("unit_read"), i * 4 + (U_FF + 2 * t + 1))
                    fn(SIL[:, t, :], ps[2 * t][:, 0:NT], ACT.Silu).then_inc(sem("silu"), 1)
            act.wait_ge(sem("down_free"), 2 + KT)
            squares(X1, SQ2)
            act.wait_ge(sem("mean_sq"), 3)
            fn(RSTD, RSTD, ACT.Sqrt).then_inc(sem("root"), 1)

        @block.vector
        def _(dve):
            tt, ts, stt, cp, red = (nc.vector.tensor_tensor, nc.vector.tensor_scalar, nc.vector.scalar_tensor_tensor,
                                    nc.vector.tensor_copy, nc.vector.tensor_reduce)
            ch = Chain(dve, "dve_chain")

            def inv_rms(n):
                dve.wait_ge(sem("squares_summed"), n + 1)
                ts(RSTD, ps[7][:, 0:NT], 1.0 / DM, EPS, ALU.mult, ALU.add).then_inc(sem("mean_sq"), 1)
                dve.wait_ge(sem("root"), n + 1)
                ch(nc.vector.reciprocal(RSTD, RSTD))

            def normed(dst, src, g, k):
                return stt(dst[:, k, 0:NT], src[:, k, :], p_(g, k), RSTD, ALU.mult, ALU.mult)

            ch(nc.vector.memset(PV[:, :, 0:1], 0.0))
            ch(nc.vector.memset(VP[:, :, 0:CH], 0.0))
            ch(nc.vector.memset(QS, 0.0))
            dve.wait_ge(sem("const_in"), 64)
            inv_rms(0)
            for k in range(KT):
                ch(normed(hT, XT, "g_mix", k))
            ch(cp(LAST[:, :, 0:1], hT[:, :, SEQ - 1:SEQ]))
            cp(LAST[:, :, 1:], hT[:, :, SEQ:NT].rearrange("p k (b t) -> p k b t", t=NS)[:, :, :, NS - 1]).then_inc(
                sem("h_done"), 1)

            def mix(u, par, dst, rows=P):
                dve.wait_ge(sem("previous"), u * 3 + 3)
                dve.wait_ge(sem("bank_free"), u + 2)
                bank = ps[par][:, 0:NT]
                ch(tt(DIF, PV[:, par, :], bank, ALU.subtract))
                mu = prm[:, bass.ds(u + PRM["mu"][0], 1)]
                stt(dst, DIF[0:rows], mu[0:rows], bank[0:rows], ALU.mult, ALU.add).then_inc(sem("bank_free"), 1)

            def flat(a):
                return a.rearrange("p a n -> p (a n)")

            mix(0, 0, SW)
            mix(1, 1, SG[:, 0, :])
            mix(2, 0, SG[:, 1, :])
            with dve.Fori(0, 4) as i:
                ch.enter(i, 4)
                for s in range(4):
                    mix(i * 4 + (U_RKV + s), (U_RKV + s) % 2, flat(RK[:, bass.ds(i * 4 + s, 1), :]))
            ch.leave(4)
            with dve.Fori(0, 2) as i:
                ch.enter(i, 4)
                for s in range(4):
                    mix(i * 4 + (U_RKV + 2 * CT + s), (U_RKV + s) % 2, flat(V[:, bass.ds(i * 4 + s, 1), :]))
            ch.leave(2)
            dve.wait_ge(sem("bank_free"), 2 + 27)

            full = [P, CT, NT]
            ch(tt(KK, K, bc(p_("k_k", 0, CT), full), ALU.mult))
            tt(BV, KK, KK, ALU.mult).then_inc(sem("kk_sq"), 1)
            for j in range(CT):
                dve.wait_ge(sem("norm"), j + 1)
                ts(BV[:, j, :], ps[2 + j % 4][:, 0:NT], 1e-24, None, ALU.max).then_inc(sem("norm_out"), 1)
            dve.wait_ge(sem("kk_root"), 1)
            ch(nc.vector.reciprocal(BV, BV))
            ch(tt(KK, KK, BV, ALU.mult))
            dve.wait_ge(sem("lora_out"), 2 * CT)
            ch(tt(BV, KK, AA, ALU.mult))
            ch(stt(AA, AA, -1.0, bc(p_("k_a", 0, CT), full), ALU.add, ALU.mult))
            ch(stt(K, AA, 1.0, K, ALU.add, ALU.mult))
            ch(tt(AA, R, K, ALU.mult))
            tt(AA, AA, bc(p_("r_k", 0, CT), full), ALU.mult).then_inc(sem("rk_done"), 1)

            dve.wait_ge(sem("dec_done"), 1)
            dve.wait_ge(sem("shift_out"), 16)
            keep = c_("keep").unsqueeze(1).broadcast_to([P, CT, SEQ])
            ch(tt(D0, DEC[:, :, 0:SEQ], keep, ALU.mult))
            ch(tt(D1, DEC[:, :, 0:SEQ], D0, ALU.subtract))
            ch(nc.vector.tensor_tensor_scan(flat(PD), flat(D0), flat(D1), 0.0, ALU.mult, ALU.add))

            def chunks(a):
                return a[:, :, 0:SEQ].rearrange("p j (c t) -> p c j t", t=CH)

            ch(cp(PC, PD.rearrange("p j (c t) -> p j c t", t=CH)[:, :, :, CH - 1]))
            for c in range(NCH):
                w = slice(c * CH, (c + 1) * CH)
                ch(tt(ARt[:, c, :, CH:64], R[:, :, w], PD[:, :, w], ALU.mult))
                ch(stt(ARt[:, c, :, 1:CH], KK[:, :, c * CH + 1:(c + 1) * CH], -1.0,
                       PD[:, :, c * CH:(c + 1) * CH - 1], ALU.mult, ALU.mult))
                ch(ts(ARt[:, c, :, 0:1], KK[:, :, c * CH:c * CH + 1], -1.0, None, ALU.mult))
            ch(nc.vector.reciprocal(PI, PD))
            for c in range(NCH):
                w = slice(c * CH, (c + 1) * CH)
                ch(tt(BKt[:, c, :, 0:CH], BV[:, :, w], PI[:, :, w], ALU.mult))
                ins = tt(BKt[:, c, :, CH:64], K[:, :, w], PI[:, :, w], ALU.mult)
                if c < NCH - 1:
                    ch(ins)
            ins.then_inc(sem("arbk_done"), 1)
            for j in range(CT):
                dve.wait_ge(sem("bonus"), j + 1)
                tt(AA[:, j, :], V[:, j, :], ps[2 + j % 4][:, 0:NT], ALU.mult).then_inc(sem("bonus_out"), 1)

            for j in range(5):
                dve.wait_ge(sem("rope_idx"), j + 1)
                x = IDXT[:, j, :]
                ch(tt(ROPI[:, 0, :], ps[6 + j % 2][:, 0:NT], c_("sinI"), ALU.mult))
                ch(tt(ROPI[:, 1, :], x, c_("cosI"), ALU.mult))
                tt(x, ROPI[:, 0, :], ROPI[:, 1, :], ALU.add).then_inc(sem("rope_idx_out"), 1)
                dve.wait_ge(sem("rope_idx_out"), j + 1)
            dve.wait_ge(sem("wi"), 1)
            ch(ts(WR, ps[6][:, 0:2 * IH].rearrange("p (a h) -> p a h", h=IH), WI_SCALE, None, ALU.mult))
            stt(WS[0:NSAMP], ps[6][0:NSAMP, 64:64 + NSAMP], WI_SCALE, c_("dmask")[0:NSAMP], ALU.mult,
                ALU.mult).then_inc(sem("wi_out"), 1)

            gmask = c_("gmask").unsqueeze(1).broadcast_to([P, CT, 64])
            for c in range(NCH):
                dve.wait_ge(sem("gram"), c + 1)
                if c >= 2:
                    dve.wait_ge(sem(f"gram_stored{c % 2}"), 16 * (c // 2))
                tt(GS[:, c % 2, :].rearrange("p (j n) -> p j n", n=64),
                   ps[2 + c % 2][:, :].rearrange("p (j n) -> p j n", n=64), gmask, ALU.mult).then_inc(
                    sem("gram_out"), 1)

            for n in range(2 * IH):
                qt, h = n // IH, n % IH
                dve.wait_ge(sem("pidx_relu"), n + 1)
                if n:
                    dve.wait_ge(sem("pidx_sum"), n)
                acc = SCP[:, qt, :]
                stt(acc, RL2[:, n % 2, :], WR[:, qt, h:h + 1],
                    c_("negtri")[:, qt * SEQ:(qt + 1) * SEQ] if h == 0 else acc, ALU.mult, ALU.add).then_inc(
                    sem("pidx_sum"), 1)
            dve.wait_ge(sem("pidx_sum"), 2 * IH)
            dve.sem_inc(sem("sc_out"), 1)

            def scores_out(b):
                dve.wait_ge(sem("sidx_sum"), b + 1)
                for half in range(2):
                    ch(cp(SC4[0:NS, half * 512:(half + 1) * 512], ps[5 + half][0:NS, :]))
                tt(SC4[0:NS, PAST:], ps[7][0:NS, 0:NS], c_("negblk")[0:NS, 0:NS], ALU.add).then_inc(sem("sc_out"), 1)

            scores_out(0)
            with dve.Fori(0, NB - 1) as b:
                ch.enter(b, 2)
                dve.wait_ge(sem("sc_stored"), b * 16 + 16)
                scores_out(b + 1)
            ch.leave(NB - 1)

            dve.wait_ge(sem("gl_in"), 32 * NCH)
            ch(nc.vector.memset(TI, 0.0))
            ch(nc.vector.memset(TI.rearrange("p a b -> p (a b)")[:, 0:CH * CH:CH + 1], 1.0))
            for t in range(1, CH):
                col = GL[:, 0:t, t:t + 1].rearrange("p s a -> p a s").broadcast_to([P, t, t])
                ch(tt(TMP[:, 0:t, 0:t], TI[:, 0:t, 0:t], col, ALU.mult))
                ins = red(TI[:, 0:t, t:t + 1], TMP[:, 0:t, 0:t], AX.X, ALU.add)
                if t < CH - 1:
                    ch(ins)
            ins.then_inc(sem("inv_done"), 1)

            with dve.Fori(0, TOPK_P // 8) as i:
                ch.enter(i, 4)
                for qt in range(2):
                    settle(dve)
                    ch(nc.vector.max(out=M8[:, qt, :], in_=SCP[:, qt, :]))
                    settle(dve)
                    ch(nc.vector.match_replace(out=SCP[:, qt, :], in_to_replace=M8[:, qt, :], in_values=SCP[:, qt, :],
                                               imm_value=TAKEN))
            ch.leave(TOPK_P // 8)
            ch(ts(MP, SCP, -2e38, NEG, ALU.is_gt, ALU.mult))
            ch(tt(MP, MP, c_("negtri").rearrange("p (a n) -> p a n", n=SEQ), ALU.add))
            dve.wait_ge(sem("scs_in"), 16)
            scs = SCS[0:NSAMP]
            with dve.Fori(0, TOPK_S // 8) as i:
                ch.enter(i, 2)
                settle(dve)
                ch(nc.vector.max(out=M8[0:NSAMP, 2, :], in_=scs))
                settle(dve)
                ch(nc.vector.match_replace(out=scs, in_to_replace=M8[0:NSAMP, 2, :], in_values=scs, imm_value=TAKEN))
            ch.leave(TOPK_S // 8)
            ch(ts(scs, scs, -2e38, NEG, ALU.is_gt, ALU.mult))
            ch(nc.vector.memset(MSK0[0:NSAMP], NEG))
            ch(cp(MSK0[0:NSAMP, :, 0:2 * P], scs[:, 0:PAST].rearrange("p (j n) -> p j n", n=2 * P)))
            tt(MSK0[0:NSAMP, 0, 2 * P:].rearrange("p (b t) -> p b t", t=NS),
               scs[:, PAST:].unsqueeze(1).broadcast_to([NSAMP, NB, NS]),
               c_("negblk")[0:NSAMP, NS:].rearrange("p (b t) -> p b t", t=NS), ALU.add).then_inc(sem("mask_done"), 1)

            dve.sem_inc(sem("rope_out"), 2)
            with dve.Fori(0, HA) as i:
                ch.enter(i, 4)
                for s in range(2):
                    dve.wait_ge(sem("rope"), i * 2 + (s + 1))
                    dve.wait_ge(sem("rope_out"), i * 2 + (s + 2))
                    x = flat(QK[:, bass.ds(i * 2 + s, 1), :])
                    ch(tt(ROPT[:, 0, :], ps[6 + s][:, 0:NT], c_("sinA"), ALU.mult))
                    ch(tt(ROPT[:, 1, :], x, c_("cosA"), ALU.mult))
                    tt(x, ROPT[:, 0, :], ROPT[:, 1, :], ALU.add).then_inc(sem("rope_out"), 1)
            ch.leave(HA)
            dve.wait_ge(sem("rope_out"), 2 + 2 * HA)
            nc.vector.memset(ST, 0.0).then_inc(sem("state"), 1)
            dve.sem_inc(sem("sy_done"), 1)

            def chunk(i, s):
                n = i * 4 + s
                dve.wait_ge(sem("ta_ready"), n + 1)
                red(SA, TA, AX.X, ALU.add).then_inc(sem("sa_done"), 1)
                dve.wait_ge(sem("turned"), n + 1)
                for q in range(4):
                    a, half = q % 2, q // 2
                    cp(BR[64 * a:64 * a + 64, half * 4:half * 4 + 4, :],
                       ps[4 + half][64 * a:64 * a + 64, :].rearrange("p (j a c) -> p j a c", a=2, c=64)[:, :, a, :]
                       ).then_inc(sem("br_out"), 1)
                dve.wait_ge(sem("x_done"), n + 1)
                cp(XS[64:64 + CH], ps[2][64:64 + CH, :].rearrange("p (h c) -> p h c", c=64)).then_inc(sem("x_out"), 1)
                dve.wait_ge(sem("u_done"), n + 1)
                cp(UV[64:64 + CH], ps[4][64:64 + CH, :].rearrange("p (h c) -> p h c", c=64)).then_inc(sem("u_out"), 1)
                dve.wait_ge(sem("chunk_done"), n + 2)
                ch(tt(ST, ST, ps[7][:, :].rearrange("p (j n) -> p j n", n=64), ALU.add))
                tt(ST, ST, PC[:, :, bass.ds(n, 1)].broadcast_to([P, CT, 64]), ALU.mult).then_inc(sem("state"), 1)
                dve.wait_ge(sem("ty_ready"), n + 1)
                red(SY[:, s, bass.ds(i * 32, 32)], TY, AX.X, ALU.add).then_inc(sem("sy_done"), 1)

            with dve.Fori(0, 2) as i:
                ch.enter(i, 4)
                for s in range(4):
                    chunk(i, s)
            ch.leave(2)

            dve.wait_ge(sem("yT"), 1)
            cp(YT[:, :, SEQ:NT], ps[2][:, 0:CT * NSAMP].rearrange("p (j n) -> p j n", n=NSAMP)).then_inc(
                sem("yT_out"), 1)
            for j in range(CT):
                dve.wait_ge(sem("mean"), j + 1)
                stt(YD[:, j, :], ps[3 + j % 4][:, 0:NT], -1.0 / DB, YT[:, j, :], ALU.mult, ALU.add).then_inc(
                    sem("mean_out"), 1)
            dve.wait_ge(sem("mean_out"), CT)
            tt(Y2, YD, YD, ALU.mult).then_inc(sem("y_sq"), 1)
            for j in range(CT):
                dve.wait_ge(sem("gate"), j + 1)
                cp(YT[:, j, :], ps[3 + j % 4][:, 0:NT]).then_inc(sem("gate_out"), 1)
            for j in range(CT):
                dve.wait_ge(sem("var"), j + 1)
                ts(Y2[:, j, :], ps[3 + j % 4][:, 0:NT], 1.0 / DB, LNX_EPS, ALU.mult, ALU.add).then_inc(
                    sem("var_out"), 1)
            dve.wait_ge(sem("var_root"), 1)
            ch(nc.vector.reciprocal(Y2, Y2))
            ch(tt(YD, YD, Y2, ALU.mult))
            ch(tt(YD, YD, bc(p_("lnx_w", 0, CT), full), ALU.mult))
            ch(tt(YD, YD, bc(p_("lnx_b", 0, CT), full), ALU.add))
            ch(tt(YD, YD, AA, ALU.add))
            tt(YT, YD, YT, ALU.mult).then_inc(sem("ob_done"), 1)

            nc.vector.memset(QZ, 0.0).then_inc(sem("qz_zero"), 1)
            dve.wait_ge(sem("v_out"), 16)
            dve.wait_ge(sem("vrows"), 1)
            ch(cp(MSK[0:NSAMP], MSK0[0:NSAMP]))
            for n in range(2 * HA + 2):
                if n < 2 * HA:
                    dve.wait_ge(sem("ps_done"), n + 1)
                    stt(PS_[:, n % 2, :], ps[2 + n % 2][:, 0:SEQ], SCALE, MP[:, n // HA, :], ALU.mult,
                        ALU.add).then_inc(sem("ps_out"), 1)
                    dve.wait_ge(sem("ps_out"), n + 1)
                    red(ROWMAX[:, n % 2, :], PS_[:, n % 2, :], AX.X, ALU.max, negate=True).then_inc(sem("nmax"), 1)
                if 1 <= n <= 2 * HA:
                    m = n - 1
                    dve.wait_ge(sem("pexp"), m + 1)
                    ch(nc.vector.reciprocal(ROWSUM[:, m % 2, :], ROWSUM[:, m % 2, :]))
                    if m >= 2:
                        dve.wait_ge(sem("pt_done"), m - 1)
                    ts(PP[:, m % 2, :], PS_[:, m % 2, :], ROWSUM[:, m % 2, :], None, ALU.mult).then_inc(
                        sem("pp_done"), 1)
                if n >= 2:
                    m = n - 2
                    dve.wait_ge(sem("pv_prompt"), m + 1)
                    cp(OA[:, m % HA, (m // HA) * P:(m // HA + 1) * P], ps[6 + m % 2][:, 0:P]).then_inc(
                        sem("oa_prompt"), 1)

            dve.sem_inc(sem("oa_out"), 1)

            def select(b):
                tt(SEL[0:NSAMP], c_("dmask")[0:NSAMP], c_("oneseq")[0:NSAMP, bass.ds(b, 1)].broadcast_to(
                    [NSAMP, NSAMP]), ALU.mult).then_inc(sem("sel_done"), 1)

            select(0)
            with dve.Fori(0, NB) as b:
                ch.enter(b, 2)
                dve.wait_ge(sem("ss_done"), b + 1)
                red(MXC, ps[2][:, 0:2 * P + NSAMP], AX.X, ALU.max).then_inc(sem("mx_done"), 1)
                select(b + 1)
                dve.wait_ge(sem("mxT"), b + 1)
                red(NMR[0:1], ps[3][0:1, 0:P].rearrange("p (j n) -> p n j", n=NSAMP), AX.X, ALU.max,
                    negate=True).then_inc(sem("nm_done"), 1)
                dve.wait_ge(sem("mb"), b + 1)
                cp(NMX, ps[3][:, P:P + 1]).then_inc(sem("nmx_done"), 1)
                dve.wait_ge(sem("et_done"), b + 1)
                ch(cp(PTS[0:NSAMP, 2, 0:NSAMP], ps[4][0:NSAMP, 2 * P:2 * P + NSAMP]))
                cp(PTS[:, 0:2, :], ps[4][:, 0:2 * P].rearrange("p (a n) -> p a n", n=P)).then_inc(sem("pts_done"), 1)
                dve.wait_ge(sem("den"), b + 1)
                ch(nc.vector.reciprocal(RCP, ps[3][:, P + 1:P + 2]))
                tt(PICK, c_("pick"), RCP.broadcast_to([P, NSAMP]), ALU.mult).then_inc(sem("pick_done"), 1)
                dve.wait_ge(sem("pv_done"), b + 1)
                cp(OR[:, 0:512], ps[5][:, :]).then_inc(sem("or_done"), 1)
                dve.wait_ge(sem("os_done"), b + 1)
                cp(OA[:, :, bass.ds(b * NS + SEQ, NS)], ps[7][:, 0:NSAMP].rearrange("p (h t) -> p h t", t=NS)).then_inc(
                    sem("oa_out"), 1)
            ch.leave(NB)

            dve.sem_inc(sem("mix_free"), 2)
            with dve.Fori(0, KT // 2) as i:
                ch.enter(i, 4)
                for s in range(2):
                    n = i * 2 + s
                    dve.wait_ge(sem("gates"), i * 4 + 2 * (s + 1))
                    dve.wait_ge(sem("unit_read"), i * 4 + (U_MIX + 2 * s + 2))
                    ch(tt(T1[:, s, :], T1[:, s, :], ps[3 * s + 1][:, 0:NT], ALU.mult))
                    ch(tt(T2[:, s, :], SGB[:, s, :], ps[3 * s + 2][:, 0:NT], ALU.mult))
                    tt(flat(MIXT[:, bass.ds(n, 1), :]), T1[:, s, :], T2[:, s, :], ALU.add).then_inc(
                        sem("mix_free"), 1)
            ch.leave(KT // 2)

            dve.wait_ge(sem("x_again"), 16)
            dve.sem_inc(sem("o_free"), 2)
            with dve.Fori(0, KT // 4) as i:
                for s in range(4):
                    dve.wait_ge(sem("unit_read"), i * 4 + (U_O + s + 1))
                    x = flat(X1[:, bass.ds(i * 4 + s, 1), :])
                    tt(x, x, ps[s % 2][:, 0:NT], ALU.add).then_inc(sem("o_free"), 1)
            dve.wait_ge(sem("o_free"), 2 + KT)
            inv_rms(1)
            for k in range(KT):
                ins = normed(hT, X1, "g_ffn", k)
                if k < KT - 1:
                    ch(ins)
            ins.then_inc(sem("h_done"), 1)

            dve.sem_inc(sem("ff_free"), 2)
            with dve.Fori(0, FT // 2) as i:
                for t in range(2):
                    dve.wait_ge(sem("silu"), i * 2 + (t + 1))
                    dve.wait_ge(sem("unit_read"), i * 4 + (U_FF + 2 * t + 2))
                    tt(flat(ACTT[:, bass.ds(i * 2 + t, 1), :]), SIL[:, t, :], ps[2 * t + 1][:, 0:NT],
                       ALU.mult).then_inc(sem("ff_free"), 1)
            dve.sem_inc(sem("down_free"), 2)
            with dve.Fori(0, KT // 2) as i:
                for t in range(2):
                    dve.wait_ge(sem("unit_read"), i * 8 + (U_DOWN + 4 * t + 4))
                    x = flat(X1[:, bass.ds(i * 2 + t, 1), :])
                    tt(x, x, ps[t][:, 0:NT], ALU.add).then_inc(sem("down_free"), 1)
            dve.wait_ge(sem("down_free"), 2 + KT)
            inv_rms(2)
            for k in range(KT):
                ins = normed(SQ2, X1, "g_final", k)
                if k < KT - 1:
                    ch(ins)
            ins.then_inc(sem("y_done"), 1)

        @block.gpsimd
        def _(pool):
            tt = nc.gpsimd.tensor_tensor
            ch = Chain(pool, "pool_chain")
            pool.wait_ge(sem("h_done"), 1)
            pool.dma_start(o_shift, LAST).then_inc(sem("shift_out"), 16)
            for a in range(6):
                pool.wait_ge(sem("rows_out"), 2 * (a + 1))
                pool.dma_start(rows_d[a], RW[0:NSAMP, a % 2, :]).then_inc(sem(f"rows_stored{a % 2}"), 16)
            pool.wait_ge(sem("arbk_done"), 1)
            for a, src in enumerate((ARt, BKt)):
                pool.dma_start(arbk_d[a].rearrange("c p n -> p c n"),
                               src.rearrange("p c j n -> p c (j n)")).then_inc(sem("arbk_stored"), 16)
            pool.wait_ge(sem("rope_idx_out"), 5)
            pool.dma_start(o_ki, KI[0:IDIM, :]).then_inc(sem("ki_out"), 16)
            for c in range(NCH):
                pool.wait_ge(sem("gram_out"), c + 1)
                pool.dma_start(gram_d[c], GS[:, c % 2, :]).then_inc(sem(f"gram_stored{c % 2}"), 16)

            def ki_pages(b, s):
                for p in range(NPG):
                    page = pool.value_load(ptab[0:1, bass.ds(b * NPG + p, 1)], min_val=0, max_val=POOL - 1)
                    pool.dma_start(KIB[:, s, p * P:(p + 1) * P], ki_d[bass.ds(page, 1)].rearrange(
                        "a p n -> p (a n)")).then_inc(sem(f"ki_in{s}"), 16)

            pool.wait_ge(sem("arbk_stored"), 32)
            pool.wait_ge(sem("const_in"), 64)
            ki_pages(0, 0)
            ki_pages(1, 1)
            for par in range(2):
                pool.wait_ge(sem(f"gram_stored{par}"), 16 * NCH // 2)
            for c in range(NCH):
                for a in range(2):
                    at = c * HB + a * CT
                    pool.dma_start(GL[at:at + CT], gram_d[c, 64 * a:64 * a + CH, :].rearrange(
                        "s (j t) -> j s t", t=64)[:, :, 0:CH]).then_inc(sem("gl_in"), 16)

            def store_scores(b):
                pool.wait_ge(sem("sc_out"), b + 2)
                pool.dma_start(sc_d[bass.ds(b * NS, NS), :], SC4[0:NS, :]).then_inc(sem("sc_stored"), 16)

            with pool.Fori(0, NB // 2 - 1) as i:
                for s in range(2):
                    store_scores(i * 2 + s)
                    ki_pages(i * 2 + (s + 2), s)
            store_scores(NB - 2)
            store_scores(NB - 1)
            pool.wait_ge(sem("sc_stored"), 16 * NB)
            pool.dma_start(SCS[0:NSAMP, :], sc_d[:, :]).then_inc(sem("scs_in"), 16)
            for par in range(2):
                pool.wait_ge(sem(f"rows_stored{par}"), 16 * 3)
            pool.wait_ge(sem("ki_out"), 16)
            for b in range(NB):
                for a in range(6):
                    pool.dma_start(SR[b * HB:(b + 1) * HB, a], rows_d[a, b * NS:(b + 1) * NS, :].rearrange(
                        "t (h j) -> h t j", j=DB)).then_inc(sem("sr_in"), 16)
            pool.wait_ge(sem("inv_done"), 1)
            for c in range(NCH):
                for a in range(2):
                    at = c * HB + a * CT
                    pool.dma_start(inv_d[c, a].rearrange("s j t -> j s t"), TI[at:at + CT]).then_inc(
                        sem("inv_stored"), 16)
            pool.wait_ge(sem("sr_in"), 16 * 6 * NB)

            def rows(a, s):
                return SR[:, a, s, :].unsqueeze(1).broadcast_to([P, 32, 64])

            with pool.Fori(0, 2) as i:
                ch.enter(i, 4 * 5)
                pool.dma_start(S2, wkv_d[:, bass.ds(i * 32, 32), :]).then_inc(sem("s2_in"), 16)
                pool.wait_ge(sem("s2_in"), i * 16 + 16)
                for s in range(NS):
                    n = i * 4 + s
                    tt(TA, S2, rows(4, s), ALU.mult).then_inc(sem("ta_ready"), 1)
                    pool.wait_ge(sem("ta_ready"), n + 1)
                    ch(tt(S2, S2, rows(1, s), ALU.mult))
                    pool.wait_ge(sem("sa_done"), n + 1)
                    ch(tt(TA, SA.unsqueeze(2).broadcast_to([P, 32, 64]), rows(5, s), ALU.mult))
                    ch(tt(S2, S2, TA, ALU.subtract))
                    ch(tt(TA, SR[:, 3, s, bass.ds(i * 32, 32)].unsqueeze(2).broadcast_to([P, 32, 64]), rows(2, s),
                          ALU.mult))
                    ch(tt(S2, S2, TA, ALU.add))
                    pool.wait_ge(sem("sy_done"), n + 1)
                    tt(TY, S2, rows(0, s), ALU.mult).then_inc(sem("ty_ready"), 1)
                pool.wait_ge(sem("ty_ready"), i * 4 + 4)
                settle(pool)
                pool.dma_start(o_wkvs[:, bass.ds(i * 32, 32), :], S2).then_inc(sem("wkvs_out"), 16)
                pool.wait_ge(sem("wkvs_out"), i * 16 + 16)
            ch.leave(2)
            pool.wait_ge(sem("sy_done"), 2 * NS + 1)
            for b in range(NB):
                pool.dma_start(yrow_d[b * NS:(b + 1) * NS, :].rearrange("t (h j) -> h t j", j=DB),
                               SY[b * HB:(b + 1) * HB]).then_inc(sem("yrow_stored"), 16)
            pool.wait_ge(sem("yrow_stored"), 16 * NB)
            pool.dma_start(YR[0:NSAMP], yrow_d[:, :]).then_inc(sem("yrow_in"), 16)
            pool.dma_start(G2[:, 0, :], lora_d[1]).then_inc(sem("g2_in"), 16)
            pool.dma_start(G2[0:32, 1, :], lora_d[2, 0:32]).then_inc(sem("g2_in"), 16)
            pool.wait_ge(sem("state"), NCH + 1)
            pool.dma_start(o_wkv, ST).then_inc(sem("wkv_out"), 16)
            pool.wait_ge(sem("oa_out"), NB + 1)
            pool.wait_ge(sem("qb_done"), NB + 1)
            pool.dma_start(XR, xT[:, :, 0:NT]).then_inc(sem("x_again"), 16)


def kernel(**inputs):
    import concourse.bacc as _bacc
    from concourse.bass_utils import run_bass_kernel_spmd as _run

    a = {k: np.asarray(v) for k, v in inputs.items()}
    f32 = np.float32

    def tiles_of(w):
        k, n = w.shape
        return w.reshape(k // P, P, n // P, P).transpose(2, 1, 0, 3).reshape(n // P, P, -1)

    def cols(v):
        return v.reshape(-1, P).T

    w_in = a["w_in"][0]
    n_in_a = w_in.shape[1] - 3360
    wa, wb = w_in[:, :n_in_a], w_in[:, n_in_a:]

    def padded(w, n):
        return np.concatenate([w, np.zeros((w.shape[0], n - w.shape[1]), f32)], 1)

    small = padded(wb[:, 3072:], 3 * P)
    ki, wi = wa[:, 3584:3648], wa[:, 3648:3656]
    idx = np.concatenate([wa[:, 3072:3584], ki, ki, padded(wi, P)], 1)
    ga, gb = wa[:, 3656:5704], wa[:, 5704:]
    pa, pb = tiles_of(a["w_pa"][0]), tiles_of(a["w_pb"][0])
    mixu = np.stack([tiles_of(gb), np.concatenate([pa, pb], 2)], 1).reshape(2 * KT, P, -1)
    ffu = np.stack([tiles_of(a["w_gate"][0]), tiles_of(a["w_up"][0])], 1).reshape(2 * FT, P, -1)
    wst = np.concatenate([tiles_of(small), tiles_of(wb[:, :3072]), tiles_of(idx), tiles_of(wa[:, :3072]), tiles_of(ga),
                          mixu, tiles_of(a["w_o"][0]), ffu], 0)
    wd = a["w_down"][0].reshape(4, FQ, P, KT, P).transpose(3, 0, 2, 1, 4).reshape(4 * KT, P, FQ * P)
    x = np.concatenate([a["x_prompt"][0], a["x_sample"].reshape(NSAMP, DM), a["state_shift"][0]], 0)
    xT = x.T.reshape(KT, P, NX).transpose(1, 0, 2)
    mu = a["mu_b"][0]
    mu = np.concatenate([mu[3072:], np.zeros(3 * P - 288, f32), mu[:3072]])
    prm = np.concatenate([cols(a["g_mix"]), cols(a["g_ffn"]), cols(a["g_final"]), cols(mu)]
                         + [cols(a[n]) for n in ("w0", "a0", "k_k", "k_a", "r_k", "lnx_w", "lnx_b")], 1)
    g2 = a["g2"][0]
    lora = np.stack([np.concatenate([a["w2"][0], a["a2"][0]], 0), g2[:P],
                     np.concatenate([g2[P:], np.zeros((2 * P - 160, 1024), f32)], 0)], 0)
    kT = a["cache_k"][0].transpose(0, 3, 2, 1).reshape(POOL, P, HA * P)
    vc = a["cache_v"][0].reshape(POOL, P, HA * P)
    kic = a["cache_kidx"][0].transpose(0, 2, 1)
    kic = np.concatenate([kic, kic], 1)
    wkv = a["state_wkv"][0].reshape(NB * HB, DB, DB)
    ins = dict(wst=wst, wdn=wd, xT=xT, cst=constants(), prm=prm, lora=lora, kT=kT, v=vc, ki=kic, wkv=wkv,
               pt=a["page_table"].reshape(1, -1))
    outs = dict(y=(P, KT, NT), k=(P, HA, NT), v=(P, HA, NT), ki=(IDIM, NT), wkv=(P, CT, DB), shift=(P, KT, 1 + NB),
                wkvs=(P, DB, DB))

    nc = _bacc.Bacc("TRN2", target_bir_lowering=False, num_devices=1)
    arrays, args = {}, []
    for name, v in ins.items():
        v = np.ascontiguousarray(v)
        arrays[f"in_{name}"] = v
        args.append(nc.dram_tensor(f"in_{name}", v.shape, mybir.dt.from_np(v.dtype), kind="ExternalInput").ap())
    for name, shape in outs.items():
        args.append(nc.dram_tensor(f"out_{name}", shape, F32, kind="ExternalOutput").ap())
    program(nc, *args)
    r = _run(nc, [arrays], core_ids=[0]).results[0]
    o = {n: np.asarray(r[f"out_{n}"]) for n in outs}

    y = o["y"].transpose(2, 1, 0).reshape(NT, DM)
    k, v = (o[n].transpose(2, 1, 0) for n in ("k", "v"))
    ki = o["ki"].T
    wkvp = o["wkv"].reshape(2, DB, CT, DB).transpose(2, 0, 3, 1).reshape(1, 1, HB, DB, DB)
    sh = o["shift"].transpose(2, 1, 0).reshape(1 + NB, DM)
    return (y[:SEQ].reshape(1, SEQ, DM), y[SEQ:].reshape(NB, NS, DM),
            k[:SEQ].reshape(1, 1, SEQ, HA, DH), v[:SEQ].reshape(1, 1, SEQ, HA, DH), ki[:SEQ].reshape(1, 1, SEQ, IDIM),
            wkvp, sh[:1].reshape(1, 1, DM),
            k[SEQ:].reshape(1, NB, NS, HA, DH), v[SEQ:].reshape(1, NB, NS, HA, DH),
            ki[SEQ:].reshape(1, NB, NS, IDIM), o["wkvs"].reshape(1, NB, HB, DB, DB), sh[1:].reshape(1, NB, DM))
```

```python
from contextlib import ExitStack

import numpy as np

import concourse.bass as bass
from concourse import mybir

F32 = mybir.dt.float32
F32R = mybir.dt.float32r
I32 = mybir.dt.int32
ALU = mybir.AluOpType
ACT = mybir.ActivationFunctionType
AX = mybir.AxisListType

P = 128
DM, SEQ, NB, NS, PAST, PAGE = 2048, 256, 8, 4, 1024, 128
NSAMP = NB * NS
NT = SEQ + NSAMP
NX = NT + NB
KT = DM // P
HA, DH = 8, 128
IH, IDIM = 8, 64
HB, DB = 16, 64
CT = HB * DB // P
DFF = 5632
FT = DFF // P
FQ = FT // 4
NPG = PAST // PAGE
CH = 32
NCH = SEQ // CH
TOPK_P, TOPK_S = 64, 256
POOL = (NB * NPG) + (NB * NPG) // 4
EPS, LNX_EPS = 1e-6, 64e-5
SCALE = DH ** -0.5
WI_SCALE = IH ** -0.5 * IDIM ** -0.5
NEG, TAKEN = -1e30, -3e38
E_HALF = float(np.exp(-0.5))

U_SMALL, U_RKV, U_IDX, U_QKV, U_GA, U_MIX, U_O, U_FF = 0, 3, 27, 33, 57, 73, 105, 121
U_DOWN = U_FF + 2 * FT
U_END = U_DOWN + 4 * KT

CONST = {}
_at = 0
for _n, _w in (("ident", 128), ("ones", 128), ("blk", 128), ("ropeA", 128), ("cosA", NT), ("sinA", NT),
               ("ropeI", 128), ("cosI", NT), ("sinI", NT), ("gmask", 64), ("negtri", 512),
               ("negblk", 36), ("spread", 32), ("dmask", 32), ("oneseq", NB + 1), ("pick", NSAMP),
               ("keep", SEQ)):
    CONST[_n] = (_at, _w)
    _at += _w
NCONST = _at
PRM = {}
_at = 0
for _n, _w in (("g_mix", 16), ("g_ffn", 16), ("g_final", 16), ("mu", 27), ("w0", 8), ("a0", 8), ("k_k", 8),
               ("k_a", 8), ("r_k", 8), ("lnx_w", 8), ("lnx_b", 8)):
    PRM[_n] = (_at, _w)
    _at += _w
NPRM = _at


def constants():
    c = np.zeros((P, NCONST), np.float32)

    def put(name, a):
        at, w = CONST[name]
        c[: a.shape[0], at:at + a.shape[1]] = a

    put("ident", np.eye(P))
    put("ones", np.ones((P, P)))
    put("blk", np.kron(np.eye(2), np.ones((64, 64))))
    pos = np.concatenate([np.arange(SEQ), np.tile(PAST + np.arange(NS), NB)]).astype(np.float32)
    for name, d, reps in (("A", DH, 1), ("I", IDIM, 2)):
        rot = d // 4
        half = rot // 2
        inv = np.float32(500000.0) ** (-np.arange(half, dtype=np.float32) * np.float32(2.0) / np.float32(rot))
        ang = inv.astype(np.float32)[:, None] * pos[None, :]
        cos, sin = np.ones((d, NT), np.float32), np.zeros((d, NT), np.float32)
        cos[:half] = cos[half:rot] = np.cos(ang)
        sin[:half] = sin[half:rot] = np.sin(ang)
        r = np.zeros((d, d), np.float32)
        for j in range(half):
            r[j, j + half] = -1.0
            r[j + half, j] = 1.0
        put("rope" + name, np.kron(np.eye(reps), r).T)
        put("cos" + name, np.tile(cos, (reps, 1)))
        put("sin" + name, np.tile(sin, (reps, 1)))
    s, t = np.arange(CH)[:, None], np.arange(CH)[None, :]
    put("gmask", np.tile(np.concatenate([s < t, s <= t], 1).astype(np.float32), (4, 1)))
    q, k = np.arange(SEQ)[:, None], np.arange(SEQ)[None, :]
    put("negtri", np.where(k > q, NEG, 0.0).reshape(2, P, SEQ).transpose(1, 0, 2).reshape(P, -1))
    b, tt = np.arange(NSAMP) // NS, np.arange(NSAMP) % NS
    future = np.where(np.arange(NS)[None, :] > tt[:, None], NEG, 0.0)
    other = np.where((b[:, None] != b[None, :]) | (tt[None, :] > tt[:, None]), NEG, 0.0)
    put("negblk", np.concatenate([future, other], 1))
    put("spread", np.repeat(np.eye(IH), NS, axis=1))
    put("dmask", (tt[:, None] == tt[None, :]).astype(np.float32))
    put("oneseq", (b[:, None] == np.arange(NB)[None, :]).astype(np.float32))
    put("pick", np.tile(np.eye(NSAMP), (4, 1)))
    put("keep", np.tile((np.arange(SEQ) % CH != 0).astype(np.float32), (P, 1)))
    return c


def program(nc, wst, wdn, xT, cst_d, prm_d, lora_d, kT_d, v_d, ki_d, wkv_d, pt_d, o_y, o_k, o_v, o_ki, o_wkv,
            o_shift, o_wkvs):
    with ExitStack() as ctx:
        offset = {}

        def sb(name, shape, dt=F32):
            offset[name] = (nc.sbuf_base + 31) // 32 * 32
            return ctx.enter_context(nc.sbuf_tensor(name, shape, dt))

        sems = {}

        def sem(name):
            if name not in sems:
                sems[name] = ctx.enter_context(nc.semaphore(name))
            return sems[name]

        cst, prm = sb("cst", [P, NCONST]), sb("prm", [P, NPRM])
        ring = sb("ring", [P, 4, KT, P])
        hT = sb("hT", [P, KT, NX])
        ar = sb("arena", [P, 35520])
        ptab = sb("ptab", [1, NB * NPG], I32)
        small = sb("small", [P, 1420])

        def c_(name):
            at, w = CONST[name]
            return cst[:, at:at + w]

        def p_(name, j, n=1):
            at, w = PRM[name]
            return prm[:, at + j:at + j + n]

        def area(at, *shape):
            n = int(np.prod(shape))
            v = ar[:, at:at + n]
            if len(shape) == 2:
                v = v.rearrange("p (a b) -> p a b", b=shape[1])
            if len(shape) == 3:
                v = v.rearrange("p (a b c) -> p a b c", b=shape[1], c=shape[2])
            return v

        R, K, VP = area(0, CT, NT), area(2304, CT, NT), area(4608, CT, CH + NT)
        V = VP[:, :, CH:]
        AA, DEC, KK, BV = area(7168, CT, NT), area(9472, CT, NT), area(11776, CT, NT), area(14080, CT, NT)
        ARt, BKt = area(16384, NCH, CT, 64), area(20480, NCH, CT, 64)
        Q, KA, VA = area(24576, HA, NT), area(26880, HA, NT), area(29184, HA, NT)
        QK = area(24576, 2 * HA, NT)
        QI, KI, WI = area(31488, 4, NT), area(32640, NT), area(32928, NT)
        IDXT = area(31488, 5, NT)
        YT = area(33216, CT, NT)
        RSTD = area(33216, NT)
        XT = area(16384, KT, NT)
        SQ = area(24576, KT, NT)
        PV = area(20480 + 1024, 2, NT)
        LORA = area(20480 + 1024 + 2 * NT, 1024)
        SW = area(20480 + 2048 + 2 * NT, NT)
        DIF = area(20480 + 2048 + 3 * NT, NT)
        RK = area(0, 2 * CT, NT)
        LAST = area(16384 + 4608, KT, 1 + NB)
        ROPI, ROPT = area(0, 2, NT), area(22528, 2, NT)
        D0, D1 = area(16384, CT, SEQ), area(16384 + SEQ * CT, CT, SEQ)
        PD, PI = area(24576, CT, SEQ), area(26880, CT, SEQ)
        RW = area(29184, 2, HB * DB)
        SCP = area(0, 2, SEQ)
        SCS = area(512, PAST + NS)
        RL = area(1540, PAST + NS)
        RL2 = area(1540, 2, SEQ)
        SC4 = area(2568, PAST + NS)
        KIB = area(16384, 2, PAST)
        sm_at = [0]

        def sml(*shape):
            n = int(np.prod(shape))
            v = small[:, sm_at[0]:sm_at[0] + n]
            sm_at[0] += n
            if len(shape) == 2:
                v = v.rearrange("p (a b) -> p a b", b=shape[1])
            if len(shape) == 3:
                v = v.rearrange("p (a b c) -> p a b c", b=shape[1], c=shape[2])
            return v


        SG = sml(2, NT)
        MP = sml(2, SEQ)
        ps = [ctx.enter_context(nc.psum_tensor(f"ps{i}", [P, 512], F32)) for i in range(8)]

        rows_d = nc.dram_tensor("sample_rows", (6, NSAMP, HB * DB), F32)
        arbk_d = nc.dram_tensor("chunk_ar_bk", (2, NCH, P, CT * 64), F32)
        gram_d = nc.dram_tensor("gram", (NCH, P, CT * 64), F32)
        inv_d = nc.dram_tensor("inverse", (NCH, 2, CH, CT, CH), F32)
        sc_d = nc.dram_tensor("sample_scores", (NSAMP, PAST + NS), F32)
        yrow_d = nc.dram_tensor("sample_y", (NSAMP, HB * DB), F32)

        WR, WS = sml(2, IH), sml(NSAMP)
        QS, WSB = sml(2, NSAMP), sml(2, NS)
        M8 = sml(3, 8)
        PC = sml(CT, NCH)
        ROWMAX, ROWSUM = sml(2, 1), sml(2, 1)
        GS = area(24576, 2, CT * 64)
        GL, TI, TMP = area(18432, CH, CH), area(19456, CH, CH), area(20480, CH, CH)
        SAR, SBK = area(16384, CT, 64), area(16896, CT, 2, 64)
        SGR, STI = area(17920, CT, 64), area(18432, CT, CH)
        SV = area(18688, CT, 2, 64)
        UV, XS, BR = area(19712, CT, 64), area(20224, CT, 64), area(20736, CT, 64)
        ST = area(22528, CT, 64)
        RP, RD = 48, 16
        S2, TA = area(9472, RP, DB), area(12544, RP, DB)
        S3, TB = area(2304, RD, DB), area(3328, RD, DB)
        SR = area(31488, 6, NS, 64)
        SY, SA, SB = area(15616, NS, 64), area(15872, RP), area(15936, RD)
        YR = area(22528 + 512, HB * DB)
        GA = area(0, KT, NT)
        OA = area(4608, HA, NT)
        VR = area(2304, 2, HA * DH)
        VS = area(29184, HA * DH)
        G2 = area(9472, 2, 1024)
        YM, YD, Y2 = area(11520, CT, NT), area(13824, CT, NT), area(11520, CT, NT)
        PS_, PP = area(16384, 2, SEQ), area(16896, 2, SEQ)
        PT = area(17408, 2, 2, P)
        KP, VG = area(7168, NPG, HA * P), area(7168 + 8192, NPG, HA * P)
        QZ = area(23552, HA * 36)
        QZH = area(23552, HA, NSAMP)
        SEL, PICK = area(23840, NSAMP), area(23872, NSAMP)
        MXC, NMR, NMX = area(23904, 1), area(23905, NSAMP), area(23937, 1)
        SUMC, RCP = area(23938, 1), area(23939, 1)
        MSK0 = area(21248, 4, 2 * P + NSAMP)
        MSK = area(30208, 4, 2 * P + NSAMP)
        ER, PTS = area(31488, 2 * P + NSAMP), area(31776, 3, P)
        OR = area(32160, HA * DH)
        MIXT = area(16384, KT, NT)
        XR = area(20992, KT, NT)
        SGB, T1, T2 = area(25600, 2, NT), area(26176, 2, NT), area(26752, 2, NT)
        SQ2 = area(0, KT, NT)
        X1 = area(20992, KT, NT)
        XF = hT[:, :, 0:NT]

        def over(name, base, at, shape, dt=F32R):
            return nc.alloc_sbuf_tensor_at(name, shape, dt, offset=offset[base] + 4 * at)

        W_HI = over("weights_hi", "arena", 30208, [P, 2, KT * P])
        W_LO = over("weights_lo", "ring", 0, [P, 4, KT * P])
        H_HI, H_LO = over("h_hi", "arena", 25600, [P, KT, NT]), over("h_lo", "hT", 0, [P, KT, NX])
        A_HI, A_LO = over("act_hi", "arena", 0, [P, FT, NT]), over("act_lo", "arena", FT * NT, [P, FT, NT])
        SIL, UG = over("silu_out", "arena", 34304, [P, 2, NT], F32), over("product", "arena", 34880, [P, 2, NT], F32)
        x1_d = nc.dram_tensor("residual", (P, KT, NT), F32)

        block = ctx.enter_context(nc.Block())

        class Chain:

            def __init__(self, eng, name):
                self.eng, self.sem, self.n, self.off = eng, sem(name), 0, 0

            def __call__(self, ins):
                ins.then_inc(self.sem, 1)
                self.n += 1
                self.eng.wait_ge(self.sem, self.off + self.n)

            def enter(self, turn, per):
                self.n0, self.per, self.off = self.n, per, turn * per

            def leave(self, turns):
                assert self.n - self.n0 == self.per, (self.n - self.n0, self.per)
                self.n, self.off = self.n0 + self.per * turns, 0

        def settle(eng):
            eng.sem_inc(sem("settled"), 1)

        def bc(a, shape):
            return a.unsqueeze(len(a.shape)).broadcast_to(shape)

        def recurrence(tt, ch, t, state, tmp, sums, r0, n, total):
            shape = [P, n, DB]

            def row(a):
                return SR[:, a, bass.ds(t, 1), :].broadcast_to(shape)

            ch(tt(tmp, state, row(4), ALU.mult))
            total(tmp, sums.unsqueeze(2))
            ch(tt(state, state, row(1), ALU.mult))
            ch(tt(tmp, sums.unsqueeze(2).broadcast_to(shape), row(5), ALU.mult))
            ch(tt(state, state, tmp, ALU.subtract))
            ch(tt(tmp, SR[:, 3, bass.ds(t, 1), r0:r0 + n].rearrange("p a n -> p n a").broadcast_to(shape), row(2),
                  ALU.mult))
            ch(tt(state, state, tmp, ALU.add))
            ch(tt(tmp, state, row(0), ALU.mult))
            total(tmp, SY[:, bass.ds(t, 1), r0:r0 + n].rearrange("p a n -> p n a"))

        @block.sync
        def _(sp):
            sp.dma_start(XT, xT[:, :, 0:NT]).then_inc(sem("x_in"), 16)
            sp.dma_start(cst[:, :], cst_d).then_inc(sem("const_in"), 16)
            sp.dma_start(prm[:, :], prm_d).then_inc(sem("const_in"), 16)
            sp.dma_start(hT[:, :, NT:NX], xT[:, :, NT:NX]).then_inc(sem("const_in"), 16)
            sp.dma_start(ptab[:, :], pt_d).then_inc(sem("const_in"), 16)
            sp.dma_start(LORA, lora_d[0]).then_inc(sem("lora_in"), 16)

            def unit(slot, u):
                sp.dma_start(ring[:, slot].rearrange("p k c -> p (k c)"),
                             wst[bass.ds(u, 1)].rearrange("a p n -> p (a n)")).then_inc(sem(f"w_in{slot}"), 16)

            def down_unit(slot, u):
                sp.dma_start(ring[:, slot].rearrange("p k c -> p (k c)")[:, 0:FQ * P],
                             wdn[bass.ds(u, 1)].rearrange("a p n -> p (a n)")).then_inc(sem(f"w_in{slot}"), 16)

            def units(a, b, load, shift=0):
                turns = (b - a) // 4
                if turns:
                    with sp.Fori(0, turns) as i:
                        for s in range(4):
                            sp.wait_ge(sem("unit_read"), i * 4 + (a + s - 3))
                            load((a + s) % 4, i * 4 + (a + s - shift))
                for u in range(a + 4 * turns, b):
                    sp.wait_ge(sem("unit_read"), u - 3)
                    load(u % 4, u - shift)

            for u in range(4):
                unit(u, u)
            units(4, U_GA + 12, unit)

            def k_page(b, p):
                page = sp.value_load(ptab[0:1, bass.ds(b * NPG + p, 1)], min_val=0, max_val=POOL - 1)
                sp.dma_start(KP[:, p], kT_d[bass.ds(page, 1)].rearrange("a p n -> p (a n)")).then_inc(
                    sem(f"k_in{p // 4}"), 16)

            def v_page(b, p):
                page = sp.value_load(ptab[0:1, bass.ds(b * NPG + p, 1)], min_val=0, max_val=POOL - 1)
                sp.dma_start(VG[:, p], v_d[bass.ds(page, 1)].rearrange("a p n -> p (a n)")).then_inc(
                    sem(f"v_in{p // 4}"), 16)

            sp.wait_ge(sem("ob_done"), CT // 2)
            for p in range(NPG):
                k_page(0, p)
            sp.wait_ge(sem("oa_prompt"), 2 * HA)
            sp.wait_ge(sem("wkv_out"), 16)
            for p in range(NPG):
                v_page(0, p)
            with sp.Fori(0, NB - 1) as b:
                sp.wait_ge(sem("ss_done"), b + 1)
                settle(sp)
                for p in range(NPG):
                    k_page(b + 1, p)
                sp.wait_ge(sem("pv_done"), b + 1)
                settle(sp)
                for p in range(NPG):
                    v_page(b + 1, p)
            units(U_GA + 20, U_DOWN, unit)
            units(U_DOWN, U_END, down_unit, U_DOWN)
            sp.wait_ge(sem("y_done"), 1)
            sp.dma_start(o_y, SQ2).then_inc(sem("y_out"), 16)
            sp.wait_ge(sem("y_out"), 16)
            for name, n in (("shift_out", 1), ("v_out", 1), ("k_out", 1), ("ki_out", 1), ("wkv_out", 1),
                            ("wkvs_out", 2)):
                sp.wait_ge(sem(name), 16 * n)

        @block.tensor
        def _(pe):
            mm, tr = nc.tensor.matmul, nc.tensor.transpose
            ident, ones, blk = c_("ident"), c_("ones"), c_("blk")

            def arrived(u0, s, i):
                pe.wait_ge(sem(f"w_in{(u0 + s) % 4}"), i * 16 + 16 * ((u0 + s) // 4 + 1))

            def tile(u0, s, i, rhs, n, k0=0, k1=KT):
                u = i * 4 + (u0 + s)
                if k0 == 0:
                    arrived(u0, s, i)
                    pe.wait_ge(sem("bank_free"), u + 1)
                slot, out = (u0 + s) % 4, ps[(u0 + s) % 2][:, 0:n]
                for k in range(k0, k1):
                    ins = mm(out, ring[:, slot, k, :], rhs(k), start=(k == 0), stop=(k == KT - 1))
                if k1 == KT:
                    ins.then_inc(sem("unit_read"), 1)

            def tiles(u0, u1, rhs, n):
                pe.wait_ge(sem("bank_free"), u0 + 2)
                turns = (u1 - u0) // 4
                if turns > 1:
                    with pe.Fori(0, turns) as i:
                        for s in range(4):
                            tile(u0, s, i, rhs, n)
                else:
                    turns = 0
                for u in range(u0 + 4 * turns, u1):
                    tile(u, 0, 0, rhs, n)

            h_all, h_tok = (lambda k: hT[:, k, :]), (lambda k: hT[:, k, 0:NT])

            def total_squares(n, src):
                for k in range(KT):
                    if k % 4 == 0:
                        pe.wait_ge(sem("squares"), 4 * n + k // 4 + 1)
                    ins = mm(ps[7][:, 0:NT], ones, src[:, k, :], start=(k == 0), stop=(k == KT - 1))
                ins.then_inc(sem("squares_summed"), 1)

            pe.sem_inc(sem("bank_free"), 2)
            pe.sem_inc(sem("chunk_done"), 1)
            pe.wait_ge(sem("const_in"), 64)
            total_squares(0, SQ)
            pe.wait_ge(sem("h_done"), 1)
            tiles(0, 3, h_all, NX)
            tiles(U_RKV, U_IDX, h_all, NX)

            pe.wait_ge(sem("lora_in"), 16)
            pe.wait_ge(sem("sw_done"), 1)
            for j in range(2 * CT):
                if j >= 4:
                    pe.wait_ge(sem("lora_out"), j - 3)
                at = 64 * (j // CT)
                mm(ps[2 + j % 4][:, 0:NT], LORA[at:at + 64, (j % CT) * P:(j % CT + 1) * P], SW[at:at + 64, :],
                   start=True, stop=True).then_inc(sem("lora"), 1)
            pe.wait_ge(sem("kk_sq"), 1)
            for j in range(CT):
                pe.wait_ge(sem("lora_out"), min(16, 13 + j))
                if j >= 4:
                    pe.wait_ge(sem("norm_out"), j - 3)
                mm(ps[2 + j % 4][:, 0:NT], blk, BV[:, j, :], start=True, stop=True).then_inc(sem("norm"), 1)
            tiles(U_IDX, U_QKV, h_tok, NT)
            pe.wait_ge(sem("rk_done"), 1)
            pe.wait_ge(sem("norm_out"), CT)
            for j in range(CT):
                if j >= 4:
                    pe.wait_ge(sem("bonus_out"), j - 3)
                mm(ps[2 + j % 4][:, 0:NT], blk, AA[:, j, :], start=True, stop=True).then_inc(sem("bonus"), 1)
            pe.wait_ge(sem("bonus_out"), CT)
            pe.wait_ge(sem("dec_done"), 1)
            for a, src in enumerate((R, DEC, K, V, KK, BV)):
                if a >= 2:
                    pe.wait_ge(sem("rows_out"), 2 * (a - 1))
                for j in range(CT):
                    ins = tr(ps[2 + 2 * (a % 2) + j // 4][0:NSAMP, (j % 4) * P:(j % 4 + 1) * P],
                             src[:, j, SEQ:NT], ident)
                ins.then_inc(sem("rows"), 1)
            pe.wait_ge(sem("bank_free"), U_QKV + 2)
            for j in range(5):
                if j >= 2:
                    pe.wait_ge(sem("rope_idx_out"), j - 1)
                mm(ps[6 + j % 2][:, 0:NT], c_("ropeI"), IDXT[:, j, :], start=True, stop=True).then_inc(
                    sem("rope_idx"), 1)
            pe.wait_ge(sem("rope_idx_out"), 5)
            for qt in range(2):
                tr(ps[6][:, qt * IH:(qt + 1) * IH], WI[0:IH, qt * P:(qt + 1) * P], ident[0:IH, 0:IH])
            mm(ps[6][0:NSAMP, 64:64 + NSAMP], c_("spread")[0:IH, :], WI[0:IH, SEQ:NT], start=True,
               stop=True).then_inc(sem("wi"), 1)
            pe.wait_ge(sem("arbk_done"), 1)
            pe.wait_ge(sem("rows_out"), 12)
            for c in range(NCH):
                if c >= 2:
                    pe.wait_ge(sem("gram_out"), c - 1)
                for h in range(HB):
                    at, j = 64 * (h % 2), h // 2
                    ins = mm(ps[2 + c % 2][at:at + 64, j * 64:(j + 1) * 64],
                             BKt[at:at + 64, c, j, :], ARt[at:at + 64, c, j, :], start=True, stop=True)
                ins.then_inc(sem("gram"), 1)
            pe.wait_ge(sem("gram_out"), NCH)
            pe.wait_ge(sem("wi_out"), 1)
            for n in range(2 * IH):
                qt, h = n // IH, n % IH
                if n >= 4:
                    pe.wait_ge(sem("pidx_relu"), n - 3)
                at = 64 * (h % 2)
                mm(ps[2 + n % 4][:, 0:SEQ], QI[at:at + 64, h // 2, qt * P:(qt + 1) * P], KI[at:at + 64, 0:SEQ],
                   start=True, stop=True).then_inc(sem("pidx"), 1)
            pe.wait_ge(sem("pidx_relu"), 2 * IH)
            with pe.Fori(0, NB // 2) as i:
                for s in range(2):
                    pe.wait_ge(sem(f"ki_in{s}"), i * (16 * NPG) + 16 * NPG)
                    pe.wait_ge(sem("qs_done"), i * 2 + (s + 1))
                    pe.wait_ge(sem("sidx_relu"), i * 6 + 3 * (s + 1))
                    for half in range(2):
                        mm(ps[2 + half][0:NSAMP, :], QS[:, s, :], KIB[:, s, half * 512:(half + 1) * 512],
                           start=True, stop=True)
                    mm(ps[4][0:NSAMP, 0:NS], QS[:, s, :], KI[:, bass.ds(i * 2 * NS + (SEQ + s * NS), NS)],
                       start=True, stop=True).then_inc(sem("sidx"), 1)
                    pe.wait_ge(sem("sidx_relu"), i * 6 + 3 * (s + 2))
                    pe.wait_ge(sem("sc_out"), i * 2 + (s + 1))
                    settle(pe)
                    for half in range(2):
                        mm(ps[5 + half][0:NS, :], WSB[0:NSAMP, s, :], RL[0:NSAMP, half * 512:(half + 1) * 512],
                           start=True, stop=True)
                    mm(ps[7][0:NS, 0:NS], WSB[0:NSAMP, s, :], RL[0:NSAMP, PAST:PAST + NS],
                       start=True, stop=True).then_inc(sem("sidx_sum"), 1)

            tiles(U_QKV, U_GA, h_tok, NT)
            pe.wait_ge(sem("bank_free"), U_GA + 2)
            pe.wait_ge(sem("sc_out"), NB + 1)
            with pe.Fori(0, HA) as i:
                for s in range(2):
                    pe.wait_ge(sem("rope_out"), i * 2 + (s + 1))
                    mm(ps[6 + s][:, 0:NT], c_("ropeA"), QK[:, bass.ds(i * 2 + s, 1), :].rearrange("p a n -> p (a n)"),
                       start=True, stop=True).then_inc(sem("rope"), 1)
            pe.wait_ge(sem("rope_out"), 2 + 2 * HA)

            def chunk(i, s):
                n = i * 4 + s
                tile(U_GA, s, i, h_tok, NT, 0, 4)
                pe.wait_ge(sem("sbk_in"), i * 128 + 32 * (s + 1))
                pe.wait_ge(sem("sv_done"), 2 * n + 2)
                settle(pe)
                for j in range(CT):
                    tr(ps[4 + j // 4][:, (j % 4) * P:(j % 4 + 1) * P], SBK[:, j].rearrange("p a n -> p (a n)"), ident)
                for j in range(CT):
                    ins = tr(ps[2 + j // 4][:, (j % 4) * P:(j % 4 + 1) * P], SV[:, j].rearrange("p a n -> p (a n)"),
                             ident)
                ins.then_inc(sem("turned"), 1)
                tile(U_GA, s, i, h_tok, NT, 4, 8)
                pe.wait_ge(sem("sgr_in"), i * 64 + 16 * (s + 1))
                pe.wait_ge(sem("sar_in"), i * 64 + 16 * (s + 1))
                pe.wait_ge(sem("turned_out"), 4 * n + 4)
                pe.wait_ge(sem("state"), n + 1)
                settle(pe)
                for h in range(HB):
                    at, j = 64 * (h % 2), h // 2
                    out = ps[2][at:at + CH, j * 64:(j + 1) * 64]
                    mm(out, SAR[at:at + 64, j, 0:CH], ST[at:at + 64, j, :], start=True, stop=False)
                    ins = mm(out, SGR[at + CH:at + 64, j, 0:CH], UV[at + CH:at + 64, j, :], start=False, stop=True,
                             tile_position=(at + CH, at))
                ins.then_inc(sem("x_done"), 1)
                tile(U_GA, s, i, h_tok, NT, 8, 11)
                pe.wait_ge(sem("sti_in"), i * 128 + 32 * (s + 1))
                pe.wait_ge(sem("x_out"), 2 * n + 2)
                pe.wait_ge(sem("br_out"), 4 * n + 4)
                settle(pe)
                for h in range(HB):
                    at, j = 64 * (h % 2), h // 2
                    ins = mm(ps[4][at:at + CH, j * 64:(j + 1) * 64], STI[at:at + CH, j, :], XS[at:at + CH, j, :],
                             start=True, stop=True)
                ins.then_inc(sem("u_done"), 1)
                tile(U_GA, s, i, h_tok, NT, 11, 13)
                pe.wait_ge(sem("u_out"), 2 * n + 2)
                pe.wait_ge(sem("y_out_of_bank"), n + 1)
                settle(pe)
                for h in range(HB):
                    at, j = 64 * (h % 2), h // 2
                    mm(ps[6][at:at + 64, j * CH:(j + 1) * CH], ST[at:at + 64, j, :], SAR[at:at + 64, j, CH:64],
                       start=True, stop=False)
                    mm(ps[6][at:at + 64, j * CH:(j + 1) * CH], UV[at:at + 64, j, :], SGR[at:at + 64, j, CH:64],
                       start=False, stop=True)
                for h in range(HB):
                    at, j = 64 * (h % 2), h // 2
                    ins = mm(ps[7][at:at + 64, j * 64:(j + 1) * 64], BR[at:at + 64, j, :], UV[at:at + 64, j, :],
                             start=True, stop=True)
                ins.then_inc(sem("chunk_done"), 1)
                tile(U_GA, s, i, h_tok, NT, 13, KT)

            with pe.Fori(0, 2) as i:
                for s in range(4):
                    chunk(i, s)

            pe.wait_ge(sem("state"), NCH + 1)
            pe.wait_ge(sem("y_out_of_bank"), NCH + 1)
            for t in range(2):
                for h in range(HA):
                    ins = tr(ps[2 + 2 * t + h // 4][:, (h % 4) * P:(h % 4 + 1) * P], VA[:, h, t * P:(t + 1) * P], ident)
            for h in range(HA):
                ins = tr(ps[6 + h // 4][0:NSAMP, (h % 4) * P:(h % 4 + 1) * P], VA[:, h, SEQ:NT], ident)
            ins.then_inc(sem("vrows"), 1)
            pe.wait_ge(sem("vrows_out"), 6)

            def pscore(n):
                qt, h = n // HA, n % HA
                if n >= 2:
                    pe.wait_ge(sem("ps_out"), n - 1)
                mm(ps[2 + n % 2][:, 0:SEQ], Q[:, h, qt * P:(qt + 1) * P], KA[:, h, 0:SEQ],
                   start=True, stop=True).then_inc(sem("ps_done"), 1)

            def pturn(n):
                pe.wait_ge(sem("pp_done"), n + 1)
                if n >= 2:
                    pe.wait_ge(sem("pt_out"), n - 1)
                for k in range(2):
                    ins = tr(ps[4 + n % 2][:, k * P:(k + 1) * P], PP[:, n % 2, k * P:(k + 1) * P], ident)
                ins.then_inc(sem("pt_done"), 1)

            def pvalue(n):
                qt, h = n // HA, n % HA
                pe.wait_ge(sem("pt_out"), n + 1)
                if n >= 2:
                    pe.wait_ge(sem("oa_prompt"), n - 1)
                for k in range(2):
                    ins = mm(ps[6 + n % 2][:, 0:P], VR[:, k, h * P:(h + 1) * P], PT[:, n % 2, k, :],
                             start=(k == 0), stop=(k == 1))
                ins.then_inc(sem("pv_prompt"), 1)

            def y_turn(n):
                if n == 0:
                    pe.wait_ge(sem("yrow_in"), 16)
                    pe.wait_ge(sem("bank_free"), U_GA + 10)
                    for j in range(CT):
                        ins = tr(ps[1][:, j * NSAMP:(j + 1) * NSAMP], YR[0:NSAMP, j * P:(j + 1) * P],
                                 ident[0:NSAMP, 0:NSAMP])
                    ins.then_inc(sem("yT"), 1)
                for q in range(4):
                    out = ps[q % 2][:, 0:NT]
                    if n in (1, 2):
                        j = 4 * (n - 1) + q
                        pe.wait_ge(sem("yT_out"), 1)
                        if j >= 2:
                            pe.wait_ge(sem("mean_out"), j - 1)
                        mm(out, blk, YT[:, j, :], start=True, stop=True).then_inc(sem("mean"), 1)
                    if n in (3, 4):
                        j = 4 * (n - 3) + q
                        pe.wait_ge(sem("g2_in"), 32)
                        pe.wait_ge(sem("mean_out"), min(CT, 7 + j))
                        if j >= 2:
                            pe.wait_ge(sem("gate_out"), j - 1)
                        mm(out, G2[:, 0, j * P:(j + 1) * P], SG[:, 0, :], start=True, stop=False)
                        mm(out, G2[0:32, 1, j * P:(j + 1) * P], SG[0:32, 1, :], start=False, stop=True).then_inc(
                            sem("gate"), 1)
                    if n in (5, 6):
                        j = 4 * (n - 5) + q
                        pe.wait_ge(sem("y_sq"), 1)
                        pe.wait_ge(sem("gate_out"), min(CT, 7 + j))
                        if j >= 2:
                            pe.wait_ge(sem("var_out"), j - 1)
                        mm(out, blk, Y2[:, j, :], start=True, stop=True).then_inc(sem("var"), 1)

            for n in range(2 * HA + 3):
                y_turn(n)
                if n < 2 * HA:
                    pscore(n)
                if 2 <= n <= 2 * HA + 1:
                    pturn(n - 2)
                if n >= 3:
                    pvalue(n - 3)

            pe.wait_ge(sem("oa_prompt"), 2 * HA)
            pe.wait_ge(sem("var_out"), CT)

            def sequence(i, s):
                n = i * 4 + s
                pe.wait_ge(sem("qb_done"), n + 1)
                pe.wait_ge(sem("sel_done"), n + 1)
                pe.wait_ge(sem("ex_done"), n + 1)
                for a in range(2):
                    pe.wait_ge(sem(f"k_in{a}"), i * 256 + 64 * (s + 1))
                settle(pe)
                for j in range(4):
                    mm(ps[2][32 * j:32 * j + 32, 0:2 * P + NSAMP], SEL[0:NSAMP, :], MSK[0:NSAMP, j, :],
                       start=True, stop=False, skip_group_check=True)
                for h in range(HA):
                    mm(ps[2][0:32, 2 * P:2 * P + NSAMP], QZH[:, h, :], KA[:, h, SEQ:NT], start=False, stop=(h == HA - 1),
                       skip_group_check=True)
                for h in range(HA):
                    for j in range(4):
                        ins = mm(ps[2][32 * j:32 * j + 32, 0:2 * P], QZH[:, h, :],
                                 KP[:, 2 * j:2 * j + 2, h * P:(h + 1) * P], start=False, stop=(h == HA - 1),
                                 skip_group_check=True)
                ins.then_inc(sem("ss_done"), 1)
                tile(U_GA + 8, s, i, h_tok, NT, 0, 4)
                pe.wait_ge(sem("mx_done"), n + 1)
                tr(ps[3][0:1, 0:P], MXC, ident).then_inc(sem("mxT"), 1)
                tile(U_GA + 8, s, i, h_tok, NT, 4, 7)
                pe.wait_ge(sem("nm_done"), n + 1)
                settle(pe)
                for j in range(4):
                    ins = mm(ps[3][32 * j:32 * j + 32, P:P + 1], NMR[0:1, :], ones[0:1, 0:1], start=True, stop=True)
                ins.then_inc(sem("mb"), 1)
                tile(U_GA + 8, s, i, h_tok, NT, 7, 12)
                pe.wait_ge(sem("ex_done"), n + 2)
                for half in range(2):
                    tr(ps[4][:, half * P:(half + 1) * P], ER[:, half * P:(half + 1) * P], ident)
                tr(ps[4][0:NSAMP, 2 * P:2 * P + NSAMP], ER[0:NSAMP, 2 * P:], ident[0:NSAMP, 0:NSAMP]).then_inc(
                    sem("et_done"), 1)
                for j in range(4):
                    ins = mm(ps[3][32 * j:32 * j + 32, P + 1:P + 2], c_("pick"), SUMC, start=True, stop=True)
                ins.then_inc(sem("den"), 1)
                tile(U_GA + 8, s, i, h_tok, NT, 12, KT)
                pe.wait_ge(sem("pts_done"), n + 1)
                for c in range(2):
                    pe.wait_ge(sem(f"v_in{c}"), i * 256 + 64 * (s + 1))
                for half in range(2):
                    for c in range(2):
                        for j in range(4):
                            mm(ps[5 + c][32 * j:32 * j + 32, :], PTS[:, half, 32 * j:32 * j + 32],
                               VG[:, 2 * j + half, c * 512:(c + 1) * 512], start=(half == 0),
                               stop=(half == 1 and j > 0), skip_group_check=True)
                for c in range(2):
                    ins = mm(ps[5 + c][0:32, :], PTS[0:NSAMP, 2, 0:NSAMP], VS[0:NSAMP, c * 512:(c + 1) * 512],
                             start=False, stop=True, skip_group_check=True)
                ins.then_inc(sem("pv_done"), 1)
                pe.wait_ge(sem("pick_done"), n + 1)
                pe.wait_ge(sem("or_done"), i * 8 + 2 * (s + 1))
                pe.wait_ge(sem("oa_out"), n + 1)
                for h in range(HA):
                    ins = mm(ps[7][:, h * NS:(h + 1) * NS], OR[:, h * P:(h + 1) * P],
                             PICK[:, h * NS:(h + 1) * NS], start=True, stop=True)
                ins.then_inc(sem("os_done"), 1)

            with pe.Fori(0, 2) as i:
                for s in range(4):
                    sequence(i, s)

            pe.wait_ge(sem("oa_out"), NB + 1)
            pe.wait_ge(sem("bank_free"), U_MIX + 2)
            with pe.Fori(0, KT // 2) as i:
                for s in range(2):
                    u0 = U_MIX + 2 * s
                    pe.wait_ge(sem("mix_free"), i * 2 + (s + 1))
                    arrived(u0, 0, i)
                    for k in range(KT):
                        ins = mm(ps[3 * s][:, 0:NT], ring[:, u0 % 4, k, :], hT[:, k, 0:NT],
                                 start=(k == 0), stop=(k == KT - 1))
                    ins.then_inc(sem("unit_read"), 1)
                    arrived(u0, 1, i)
                    for part, src in enumerate((OA, YT)):
                        for k in range(CT):
                            ins = mm(ps[3 * s + 1 + part][:, 0:NT], ring[:, (u0 + 1) % 4, part * CT + k, :],
                                     src[:, k, :], start=(k == 0), stop=(k == CT - 1))
                    ins.then_inc(sem("unit_read"), 1)
            pe.wait_ge(sem("mix_free"), KT + 2)

            with pe.Fori(0, KT // 4) as i:
                for s in range(4):
                    arrived(U_O, s, i)
                    pe.wait_ge(sem("o_free"), i * 4 + (s + 1))
                    for k in range(KT):
                        ins = mm(ps[s % 2][:, 0:NT], ring[:, (U_O + s) % 4, k, :], MIXT[:, k, :],
                                 start=(k == 0), stop=(k == KT - 1))
                    ins.then_inc(sem("unit_read"), 1)
            total_squares(1, SQ2)

            def three(out, u, k, hi, lo, start, stop):
                w = slice(k * P, (k + 1) * P)
                mm(out, W_HI[:, (u - U_FF) % 2, w], hi, start=start, stop=False)
                mm(out, W_HI[:, (u - U_FF) % 2, w], lo, start=False, stop=False)
                return mm(out, W_LO[:, u % 4, w], hi, start=False, stop=stop)

            with pe.Fori(0, FT // 2) as i:
                for s in range(4):
                    pe.wait_ge(sem("w_split"), i * 4 + (s + 1))
                    if s % 2 == 0:
                        pe.wait_ge(sem("ff_free"), i * 2 + (s // 2 + 1))
                    for k in range(KT):
                        if s == 0 and k % 4 == 0:
                            pe.wait_ge(sem("h_split"), k // 4 + 1)
                        ins = three(ps[s][:, 0:NT], U_FF + s, k, H_HI[:, k, :], H_LO[:, k, 0:NT],
                                    k == 0, k == KT - 1)
                    ins.then_inc(sem("unit_read"), 1)
            pe.wait_ge(sem("ff_free"), FT + 2)
            pe.wait_ge(sem("act_lo"), FT + 2)
            with pe.Fori(0, KT // 2) as i:
                for t in range(2):
                    pe.wait_ge(sem("down_free"), i * 2 + (t + 1))
                    for q in range(4):
                        pe.wait_ge(sem("w_split"), i * 8 + (2 * FT + 4 * t + q + 1))
                        for k in range(FQ):
                            ins = three(ps[t][:, 0:NT], U_DOWN + 4 * t + q, k, A_HI[:, q * FQ + k, :],
                                        A_LO[:, q * FQ + k, :], q == 0 and k == 0, q == 3 and k == FQ - 1)
                        ins.then_inc(sem("unit_read"), 1)
            total_squares(2, SQ2)

        @block.scalar
        def _(act):
            fn = nc.scalar.activation
            ch = Chain(act, "act_chain")

            def squares(src, dst):
                for q in range(4):
                    fn(dst[:, 4 * q:4 * q + 4, :], src[:, 4 * q:4 * q + 4, :], ACT.Square).then_inc(sem("squares"), 1)

            act.wait_ge(sem("x_in"), 16)
            squares(XT, SQ)
            act.wait_ge(sem("mean_sq"), 1)
            fn(RSTD, RSTD, ACT.Sqrt).then_inc(sem("root"), 1)

            def previous(u, par):
                act.wait_ge(sem("unit_read"), u + 1)
                act.wait_ge(sem("bank_free"), u + 1)
                bank, pv = ps[par], PV[:, par, :]
                now = bank[:, SEQ:NT].rearrange("p (b t) -> p b t", t=NS)
                out = pv[:, SEQ:NT].rearrange("p (b t) -> p b t", t=NS)
                fn(pv[:, 1:SEQ], bank[:, 0:SEQ - 1], ACT.Copy).then_inc(sem("previous"), 1)
                fn(out[:, :, 1:NS], now[:, :, 0:NS - 1], ACT.Copy).then_inc(sem("previous"), 1)
                fn(out[:, :, 0:1], bank[:, NT:NX].rearrange("p (b t) -> p b t", t=1), ACT.Copy).then_inc(
                    sem("previous"), 1)

            for u in range(3):
                previous(u, u % 2)
            act.wait_ge(sem("bank_free"), 2 + 3)
            fn(SW[0:64, :], SW[0:64, :], ACT.Tanh).then_inc(sem("sw_done"), 1)
            ch(fn(SG, SG, ACT.Sigmoid))
            with act.Fori(0, 6) as i:
                for s in range(4):
                    previous(i * 4 + (U_RKV + s), (U_RKV + s) % 2)

            for j in range(2 * CT):
                act.wait_ge(sem("lora"), j + 1)
                dst, bias = (DEC[:, j, :], p_("w0", j)) if j < CT else (AA[:, j - CT, :], p_("a0", j - CT))
                fn(dst, ps[2 + j % 4][:, 0:NT], ACT.Sigmoid, bias=bias).then_inc(sem("lora_out"), 1)
            act.wait_ge(sem("lora_out"), 2 * CT)
            fn(DEC, DEC, ACT.Exp, scale=-E_HALF).then_inc(sem("dec_done"), 1)
            act.wait_ge(sem("norm_out"), CT)
            fn(BV, BV, ACT.Sqrt).then_inc(sem("kk_root"), 1)
            for j in range(6):
                u = U_IDX + j
                act.wait_ge(sem("unit_read"), u + 1)
                dst = QI[:, j, :] if j < 4 else (KI if j == 4 else WI)
                fn(dst, ps[u % 2][:, 0:NT], ACT.Copy).then_inc(sem("bank_free"), 1)
            for a in range(6):
                act.wait_ge(sem("rows"), a + 1)
                if a >= 2:
                    act.wait_ge(sem(f"rows_stored{a % 2}"), 16 * (a // 2))
                for half in range(2):
                    fn(RW[0:NSAMP, a % 2, half * 512:(half + 1) * 512], ps[2 + 2 * (a % 2) + half][0:NSAMP, :],
                       ACT.Copy).then_inc(sem("rows_out"), 1)
            for n in range(2 * IH):
                act.wait_ge(sem("pidx"), n + 1)
                if n >= 2:
                    act.wait_ge(sem("pidx_sum"), n - 1)
                fn(RL2[:, n % 2, :], ps[2 + n % 4][:, 0:SEQ], ACT.Relu).then_inc(sem("pidx_relu"), 1)
            act.wait_ge(sem("pidx_sum"), 2 * IH)
            act.wait_ge(sem("wi_out"), 1)
            act.sem_inc(sem("sidx_relu"), 3)
            with act.Fori(0, NB // 2) as i:
                ch.enter(i, 4)
                for s in range(2):
                    b = i * 2 + s
                    q = QS[:, s, :].rearrange("p (j a t) -> p j a t", a=2, t=NS)
                    for a in range(2):
                        ch(fn(q[64 * a:64 * a + 64, :, a, :],
                              QI[64 * a:64 * a + 64, :, bass.ds(i * 2 * NS + (SEQ + s * NS), NS)], ACT.Copy))
                    fn(WSB[0:NSAMP, s, :], WS[0:NSAMP, bass.ds(i * 2 * NS + s * NS, NS)], ACT.Copy).then_inc(
                        sem("qs_done"), 1)
                    act.wait_ge(sem("sidx"), b + 1)
                    for half in range(2):
                        fn(RL[0:NSAMP, half * 512:(half + 1) * 512], ps[2 + half][0:NSAMP, :], ACT.Relu).then_inc(
                            sem("sidx_relu"), 1)
                    fn(RL[0:NSAMP, PAST:PAST + NS], ps[4][0:NSAMP, 0:NS], ACT.Relu).then_inc(sem("sidx_relu"), 1)
            ch.leave(NB // 2)

            act.wait_ge(sem("arbk_done"), 1)
            for par in range(2):
                act.wait_ge(sem(f"rows_stored{par}"), 16 * 3)
                act.wait_ge(sem(f"gram_stored{par}"), 16 * NCH // 2)
            act.wait_ge(sem("arbk_stored"), 32)
            qkv = area(24576, 3 * HA, NT)
            with act.Fori(0, 6) as i:
                for s in range(4):
                    act.wait_ge(sem("unit_read"), i * 4 + (U_QKV + s + 1))
                    fn(qkv[:, bass.ds(i * 4 + s, 1), :].rearrange("p a n -> p (a n)"), ps[(U_QKV + s) % 2][:, 0:NT],
                       ACT.Copy).then_inc(sem("bank_free"), 1)
            act.wait_ge(sem("bank_free"), U_GA + 2)
            act.dma_start(o_v, VA).then_inc(sem("v_out"), 16)
            act.wait_ge(sem("rope_out"), 2 + 2 * HA)
            act.dma_start(o_k, KA).then_inc(sem("k_out"), 16)

            act.wait_ge(sem("inv_stored"), 32 * NCH)
            act.wait_ge(sem("mask_done"), 1)

            def stage_b(c):
                for a in range(2):
                    act.dma_start(SBK[:, :, a, :], arbk_d[1][bass.ds(c, 1)].rearrange(
                        "a p (j n) -> p (a j) n", n=64)).then_inc(sem("sbk_in"), 16)
                for a in range(2):
                    fn(SV[:, :, a, :], VP[:, :, bass.ds(c * CH, 2 * CH)], ACT.Copy).then_inc(sem("sv_done"), 1)

            def stage_inverse(c):
                for a in range(2):
                    act.dma_start(STI[64 * a:64 * a + CH].rearrange("p a b -> p (a b)"),
                                  inv_d[bass.ds(c, 1), a].rearrange("a s j t -> s (a j t)")).then_inc(
                        sem("sti_in"), 16)

            def stage_a(c):
                act.dma_start(SAR.rearrange("p a b -> p (a b)"),
                              arbk_d[0][bass.ds(c, 1)].rearrange("a p n -> p (a n)")).then_inc(sem("sar_in"), 16)
                act.dma_start(SGR.rearrange("p a b -> p (a b)"),
                              gram_d[bass.ds(c, 1)].rearrange("a p n -> p (a n)")).then_inc(sem("sgr_in"), 16)

            def chunk(i, s):
                n = i * 4 + s
                act.wait_ge(sem("turned"), n + 1)
                for q in range(4):
                    a, half = q % 2, q // 2
                    fn(UV[64 * a + CH:64 * a + 64, half * 4:half * 4 + 4, :],
                       ps[2 + half][64 * a + CH:64 * a + 64, :].rearrange("p (j a c) -> p j a c", a=2, c=64)[:, :, a, :],
                       ACT.Copy).then_inc(sem("turned_out"), 1)
                nxt = i * 4 + (s + 1) if s < 3 else -(i * 4) + 4
                stage_b(nxt)
                act.wait_ge(sem("x_done"), n + 1)
                fn(XS[0:CH], ps[2][0:CH, :].rearrange("p (h i) -> p h i", i=64), ACT.Copy).then_inc(sem("x_out"), 1)
                act.wait_ge(sem("u_done"), n + 1)
                fn(UV[0:CH], ps[4][0:CH, :].rearrange("p (h i) -> p h i", i=64), ACT.Copy).then_inc(sem("u_out"), 1)
                stage_inverse(nxt)
                act.wait_ge(sem("chunk_done"), n + 2)
                fn(YT[:, :, bass.ds(i * 4 * CH + s * CH, CH)],
                   ps[6][:, 0:CT * CH].rearrange("p (j t) -> p j t", t=CH), ACT.Copy).then_inc(
                    sem("y_out_of_bank"), 1)
                stage_a(nxt)
                act.wait_ge(sem("unit_read"), n + (U_GA + 1))
                fn(GA[:, bass.ds(n, 1), :].rearrange("p a n -> p (a n)"), ps[(U_GA + s) % 2][:, 0:NT],
                   ACT.Copy).then_inc(sem("bank_free"), 1)

            act.sem_inc(sem("y_out_of_bank"), 1)
            stage_b(0)
            stage_inverse(0)
            stage_a(0)
            with act.Fori(0, 2) as i:
                for s in range(4):
                    chunk(i, s)
            act.wait_ge(sem("vrows"), 1)
            act.wait_ge(sem("wkvs_out"), 32)
            for t in range(2):
                for half in range(2):
                    fn(VR[:, t, half * 512:(half + 1) * 512], ps[2 + 2 * t + half][:, :], ACT.Copy).then_inc(
                        sem("vrows_out"), 1)
            act.wait_ge(sem("v_out"), 16)
            for half in range(2):
                fn(VS[0:NSAMP, half * 512:(half + 1) * 512], ps[6 + half][0:NSAMP, :], ACT.Copy).then_inc(
                    sem("vrows_out"), 1)
            for n in range(2 * HA + 2):
                if n == 3:
                    act.wait_ge(sem("mean_out"), CT)
                    fn(Y2, YD, ACT.Square).then_inc(sem("y_sq"), 1)
                for j in range(4 * (n - 3), 4 * (n - 2)):
                    if n in (3, 4):
                        act.wait_ge(sem("gate"), j + 1)
                        fn(YT[:, j, :], ps[j % 2][:, 0:NT], ACT.Copy).then_inc(sem("gate_out"), 1)
                if n == 7:
                    act.wait_ge(sem("var_out"), CT)
                    fn(Y2, Y2, ACT.Sqrt).then_inc(sem("var_root"), 1)
                if n < 2 * HA:
                    act.wait_ge(sem("nmax"), n + 1)
                    fn(PS_[:, n % 2, :], PS_[:, n % 2, :], ACT.Exp, bias=ROWMAX[:, n % 2, :],
                       accum_out=ROWSUM[:, n % 2, :]).then_inc(sem("pexp"), 1)
                if n >= 2:
                    m = n - 2
                    act.wait_ge(sem("pt_done"), m + 1)
                    if m >= 2:
                        act.wait_ge(sem("pv_prompt"), m - 1)
                    fn(PT[:, m % 2, :, :], ps[4 + m % 2][:, 0:2 * P].rearrange("p (k q) -> p k q", q=P),
                       ACT.Copy).then_inc(sem("pt_out"), 1)

            def sequence(i, s):
                n = i * 4 + s
                act.wait_ge(sem("ss_done"), n + 1)
                if s < 3:
                    nxt = i * 4 * NS + (SEQ + (s + 1) * NS)
                else:
                    nxt = -(i * 4 * NS) + (SEQ + 4 * NS)
                fn(QZD, Q[:, :, bass.ds(nxt, NS)], ACT.Copy, scale=SCALE).then_inc(sem("qb_done"), 1)
                act.wait_ge(sem("nmx_done"), n + 1)
                fn(ER, ps[2][:, 0:2 * P + NSAMP], ACT.Exp, bias=NMX, accum_out=SUMC).then_inc(sem("ex_done"), 1)
                act.wait_ge(sem("unit_read"), n + (U_GA + 9))
                fn(GA[:, bass.ds(n + 8, 1), :].rearrange("p a n -> p (a n)"), ps[(U_GA + s) % 2][:, 0:NT],
                   ACT.Copy).then_inc(sem("bank_free"), 1)
                slot = (U_GA + 12 + s) % 4
                act.dma_start(ring[:, slot].rearrange("p k c -> p (k c)"),
                              wst[bass.ds(i * 4 + (U_GA + 12 + s), 1)].rearrange("a p n -> p (a n)")).then_inc(
                    sem(f"w_in{slot}"), 16)
                act.wait_ge(sem("pv_done"), n + 1)
                fn(OR[:, 512:], ps[6][:, :], ACT.Copy).then_inc(sem("or_done"), 1)

            act.wait_ge(sem("oa_prompt"), 2 * HA)
            act.wait_ge(sem("qz_zero"), 1)
            act.sem_inc(sem("ex_done"), 1)
            QZD = QZ.rearrange("p (h x) -> p h x", x=36)[:, :, 0:NS]
            fn(QZD, Q[:, :, SEQ:SEQ + NS], ACT.Copy, scale=SCALE).then_inc(sem("qb_done"), 1)
            with act.Fori(0, 2) as i:
                for s in range(4):
                    sequence(i, s)

            act.wait_ge(sem("qb_done"), NB + 1)
            with act.Fori(0, KT // 2) as i:
                for s in range(2):
                    act.wait_ge(sem("mix_free"), i * 2 + (s + 1))
                    fn(T1[:, s, :], GA[:, bass.ds(i * 2 + s, 1), :].rearrange("p a n -> p (a n)"),
                       ACT.Sigmoid).then_inc(sem("gates"), 1)
                    act.wait_ge(sem("unit_read"), i * 4 + (U_MIX + 2 * s + 1))
                    fn(SGB[:, s, :], ps[3 * s][:, 0:NT], ACT.Sigmoid).then_inc(sem("gates"), 1)

            def high(u, i=0, per=0, n=KT * P):
                act.wait_ge(sem(f"w_in{u % 4}"), i * (4 * per) + 16 * (u // 4 + 1))
                fn(W_HI[:, (u - U_FF) % 2, 0:n], ring[:, u % 4].rearrange("p k c -> p (k c)")[:, 0:n],
                   ACT.Copy).then_inc(sem("w_high"), 1)

            high(U_FF)
            high(U_FF + 1)
            act.wait_ge(sem("o_free"), 2 + KT)
            squares(X1, SQ2)
            act.wait_ge(sem("mean_sq"), 2)
            fn(SG[:, 0, :], SG[:, 0, :], ACT.Sqrt).then_inc(sem("root"), 1)
            for g in range(4):
                act.wait_ge(sem("h_done"), g + 2)
                fn(H_HI[:, 4 * g:4 * g + 4, :], hT[:, 4 * g:4 * g + 4, 0:NT], ACT.Copy).then_inc(sem("h_high"), 1)
            def product(i, t, n=KT * P):
                act.wait_ge(sem("unit_read"), i * 4 + (U_FF + 2 * t + 1))
                high(U_FF + 2 * t + 2, i, 4, n)
                act.wait_ge(sem("ff_free"), i * 2 + (t + 1))
                fn(SIL[:, t, :], ps[2 * t][:, 0:NT], ACT.Silu).then_inc(sem("silu"), 1)
                act.wait_ge(sem("unit_read"), i * 4 + (U_FF + 2 * t + 2))
                high(U_FF + 2 * t + 3, i, 4, n)
                act.wait_ge(sem("ff_free"), i * 2 + (t + 3))
                fn(A_HI[:, bass.ds(i * 2 + t, 1), :].rearrange("p a n -> p (a n)"), UG[:, t, :],
                   ACT.Copy).then_inc(sem("act_high"), 1)

            with act.Fori(0, FT // 2 - 1) as i:
                for t in range(2):
                    product(i, t)
            product(FT // 2 - 1, 0)
            product(FT // 2 - 1, 1, FQ * P)
            with act.Fori(0, KT // 2 - 1) as i:
                for q in range(8):
                    act.wait_ge(sem("unit_read"), i * 8 + (U_DOWN + q + 1))
                    high(U_DOWN + q + 2, i, 8, FQ * P)
            for u in range(U_END - 8, U_END - 2):
                act.wait_ge(sem("unit_read"), u + 1)
                high(u + 2, n=FQ * P)
            act.wait_ge(sem("down_free"), 2 + KT)
            squares(XF, SQ2)
            act.wait_ge(sem("mean_sq"), 3)
            fn(SG[:, 0, :], SG[:, 0, :], ACT.Sqrt).then_inc(sem("root"), 1)

        @block.vector
        def _(dve):
            tt, ts, stt, cp, red = (nc.vector.tensor_tensor, nc.vector.tensor_scalar, nc.vector.scalar_tensor_tensor,
                                    nc.vector.tensor_copy, nc.vector.tensor_reduce)
            ch = Chain(dve, "dve_chain")

            def inv_rms(n):
                dve.wait_ge(sem("squares_summed"), n + 1)
                rstd = RSTD if n == 0 else SG[:, 0, :]
                ts(rstd, ps[7][:, 0:NT], 1.0 / DM, EPS, ALU.mult, ALU.add).then_inc(sem("mean_sq"), 1)
                dve.wait_ge(sem("root"), n + 1)
                ch(nc.vector.reciprocal(rstd, rstd))

            def normed(dst, src, g, k):
                return stt(dst[:, k, 0:NT], src[:, k, :], p_(g, k), RSTD if g == "g_mix" else SG[:, 0, :],
                           ALU.mult, ALU.mult)

            ch(nc.vector.memset(PV[:, :, 0:1], 0.0))
            ch(nc.vector.memset(VP[:, :, 0:CH], 0.0))
            ch(nc.vector.memset(QS, 0.0))
            dve.wait_ge(sem("const_in"), 64)
            inv_rms(0)
            for k in range(KT):
                ch(normed(hT, XT, "g_mix", k))
            ch(cp(LAST[:, :, 0:1], hT[:, :, SEQ - 1:SEQ]))
            cp(LAST[:, :, 1:], hT[:, :, SEQ:NT].rearrange("p k (b t) -> p k b t", t=NS)[:, :, :, NS - 1]).then_inc(
                sem("h_done"), 1)

            def mix(u, par, dst, rows=P):
                dve.wait_ge(sem("previous"), u * 3 + 3)
                dve.wait_ge(sem("bank_free"), u + 2)
                bank = ps[par][:, 0:NT]
                ch(tt(DIF, PV[:, par, :], bank, ALU.subtract))
                mu = prm[:, bass.ds(u + PRM["mu"][0], 1)]
                stt(dst, DIF[0:rows], mu[0:rows], bank[0:rows], ALU.mult, ALU.add).then_inc(sem("bank_free"), 1)

            def flat(a):
                return a.rearrange("p a n -> p (a n)")

            mix(0, 0, SW)
            mix(1, 1, SG[:, 0, :])
            mix(2, 0, SG[:, 1, :])
            with dve.Fori(0, 4) as i:
                ch.enter(i, 4)
                for s in range(4):
                    mix(i * 4 + (U_RKV + s), (U_RKV + s) % 2, flat(RK[:, bass.ds(i * 4 + s, 1), :]))
            ch.leave(4)
            with dve.Fori(0, 2) as i:
                ch.enter(i, 4)
                for s in range(4):
                    mix(i * 4 + (U_RKV + 2 * CT + s), (U_RKV + s) % 2, flat(V[:, bass.ds(i * 4 + s, 1), :]))
            ch.leave(2)
            dve.wait_ge(sem("bank_free"), 2 + 27)

            full = [P, CT, NT]
            ch(tt(KK, K, bc(p_("k_k", 0, CT), full), ALU.mult))
            tt(BV, KK, KK, ALU.mult).then_inc(sem("kk_sq"), 1)
            for j in range(CT):
                dve.wait_ge(sem("norm"), j + 1)
                ts(BV[:, j, :], ps[2 + j % 4][:, 0:NT], 1e-24, None, ALU.max).then_inc(sem("norm_out"), 1)
            dve.wait_ge(sem("kk_root"), 1)
            ch(nc.vector.reciprocal(BV, BV))
            ch(tt(KK, KK, BV, ALU.mult))
            dve.wait_ge(sem("lora_out"), 2 * CT)
            ch(tt(BV, KK, AA, ALU.mult))
            ch(stt(AA, AA, -1.0, bc(p_("k_a", 0, CT), full), ALU.add, ALU.mult))
            ch(stt(K, AA, 1.0, K, ALU.add, ALU.mult))
            ch(tt(AA, R, K, ALU.mult))
            tt(AA, AA, bc(p_("r_k", 0, CT), full), ALU.mult).then_inc(sem("rk_done"), 1)

            dve.wait_ge(sem("dec_done"), 1)
            dve.wait_ge(sem("shift_out"), 16)
            keep = c_("keep").unsqueeze(1).broadcast_to([P, CT, SEQ])
            ch(tt(D0, DEC[:, :, 0:SEQ], keep, ALU.mult))
            ch(tt(D1, DEC[:, :, 0:SEQ], D0, ALU.subtract))
            ch(nc.vector.tensor_tensor_scan(flat(PD), flat(D0), flat(D1), 0.0, ALU.mult, ALU.add))

            def chunks(a):
                return a[:, :, 0:SEQ].rearrange("p j (c t) -> p c j t", t=CH)

            ch(cp(PC, PD.rearrange("p j (c t) -> p j c t", t=CH)[:, :, :, CH - 1]))
            for c in range(NCH):
                w = slice(c * CH, (c + 1) * CH)
                ch(tt(ARt[:, c, :, CH:64], R[:, :, w], PD[:, :, w], ALU.mult))
                ch(stt(ARt[:, c, :, 1:CH], KK[:, :, c * CH + 1:(c + 1) * CH], -1.0,
                       PD[:, :, c * CH:(c + 1) * CH - 1], ALU.mult, ALU.mult))
                ch(ts(ARt[:, c, :, 0:1], KK[:, :, c * CH:c * CH + 1], -1.0, None, ALU.mult))
            for j in range(CT):
                dve.wait_ge(sem("bonus"), j + 1)
                tt(AA[:, j, :], V[:, j, :], ps[2 + j % 4][:, 0:NT], ALU.mult).then_inc(sem("bonus_out"), 1)
            ch(nc.vector.reciprocal(PI, PD))
            for c in range(NCH):
                w = slice(c * CH, (c + 1) * CH)
                ch(tt(BKt[:, c, :, 0:CH], BV[:, :, w], PI[:, :, w], ALU.mult))
                ins = tt(BKt[:, c, :, CH:64], K[:, :, w], PI[:, :, w], ALU.mult)
                if c < NCH - 1:
                    ch(ins)
            ins.then_inc(sem("arbk_done"), 1)

            for j in range(5):
                dve.wait_ge(sem("rope_idx"), j + 1)
                x = IDXT[:, j, :]
                ch(tt(ROPI[:, 0, :], ps[6 + j % 2][:, 0:NT], c_("sinI"), ALU.mult))
                ch(tt(ROPI[:, 1, :], x, c_("cosI"), ALU.mult))
                tt(x, ROPI[:, 0, :], ROPI[:, 1, :], ALU.add).then_inc(sem("rope_idx_out"), 1)
                dve.wait_ge(sem("rope_idx_out"), j + 1)
            dve.wait_ge(sem("wi"), 1)
            ch(ts(WR, ps[6][:, 0:2 * IH].rearrange("p (a h) -> p a h", h=IH), WI_SCALE, None, ALU.mult))
            stt(WS[0:NSAMP], ps[6][0:NSAMP, 64:64 + NSAMP], WI_SCALE, c_("dmask")[0:NSAMP], ALU.mult,
                ALU.mult).then_inc(sem("wi_out"), 1)

            gmask = c_("gmask").unsqueeze(1).broadcast_to([P, CT, 64])
            for c in range(NCH):
                dve.wait_ge(sem("gram"), c + 1)
                if c >= 2:
                    dve.wait_ge(sem(f"gram_stored{c % 2}"), 16 * (c // 2))
                tt(GS[:, c % 2, :].rearrange("p (j n) -> p j n", n=64),
                   ps[2 + c % 2][:, :].rearrange("p (j n) -> p j n", n=64), gmask, ALU.mult).then_inc(
                    sem("gram_out"), 1)

            for n in range(2 * IH):
                qt, h = n // IH, n % IH
                dve.wait_ge(sem("pidx_relu"), n + 1)
                if n:
                    dve.wait_ge(sem("pidx_sum"), n)
                acc = SCP[:, qt, :]
                stt(acc, RL2[:, n % 2, :], WR[:, qt, h:h + 1],
                    c_("negtri")[:, qt * SEQ:(qt + 1) * SEQ] if h == 0 else acc, ALU.mult, ALU.add).then_inc(
                    sem("pidx_sum"), 1)
            dve.wait_ge(sem("pidx_sum"), 2 * IH)
            dve.sem_inc(sem("sc_out"), 1)

            def scores_out(b):
                dve.wait_ge(sem("sidx_sum"), b + 1)
                for half in range(2):
                    ch(cp(SC4[0:NS, half * 512:(half + 1) * 512], ps[5 + half][0:NS, :]))
                tt(SC4[0:NS, PAST:], ps[7][0:NS, 0:NS], c_("negblk")[0:NS, 0:NS], ALU.add).then_inc(sem("sc_out"), 1)

            scores_out(0)
            with dve.Fori(0, NB - 1) as b:
                ch.enter(b, 2)
                dve.wait_ge(sem("sc_stored"), b * 16 + 16)
                scores_out(b + 1)
            ch.leave(NB - 1)

            dve.wait_ge(sem("gl_in"), 32 * NCH)
            ch(nc.vector.memset(TI, 0.0))
            ch(nc.vector.memset(TI.rearrange("p a b -> p (a b)")[:, 0:CH * CH:CH + 1], 1.0))
            for t in range(1, CH):
                col = GL[:, 0:t, t:t + 1].rearrange("p s a -> p a s").broadcast_to([P, t, t])
                ch(tt(TMP[:, 0:t, 0:t], TI[:, 0:t, 0:t], col, ALU.mult))
                ins = red(TI[:, 0:t, t:t + 1], TMP[:, 0:t, 0:t], AX.X, ALU.add)
                if t < CH - 1:
                    ch(ins)
            ins.then_inc(sem("inv_done"), 1)

            with dve.Fori(0, TOPK_P // 8) as i:
                ch.enter(i, 4)
                for qt in range(2):
                    settle(dve)
                    ch(nc.vector.max(out=M8[:, qt, :], in_=SCP[:, qt, :]))
                    settle(dve)
                    ch(nc.vector.match_replace(out=SCP[:, qt, :], in_to_replace=M8[:, qt, :], in_values=SCP[:, qt, :],
                                               imm_value=TAKEN))
            ch.leave(TOPK_P // 8)
            ch(ts(MP, SCP, -2e38, NEG, ALU.is_gt, ALU.mult))
            ch(tt(MP, MP, c_("negtri").rearrange("p (a n) -> p a n", n=SEQ), ALU.add))
            dve.wait_ge(sem("scs_in"), 16)
            scs = SCS[0:NSAMP]
            with dve.Fori(0, TOPK_S // 8) as i:
                ch.enter(i, 2)
                settle(dve)
                ch(nc.vector.max(out=M8[0:NSAMP, 2, :], in_=scs))
                settle(dve)
                ch(nc.vector.match_replace(out=scs, in_to_replace=M8[0:NSAMP, 2, :], in_values=scs, imm_value=TAKEN))
            ch.leave(TOPK_S // 8)
            ch(ts(scs, scs, -2e38, NEG, ALU.is_gt, ALU.mult))
            ch(nc.vector.memset(MSK0[0:NSAMP], NEG))
            ch(cp(MSK0[0:NSAMP, :, 0:2 * P], scs[:, 0:PAST].rearrange("p (j n) -> p j n", n=2 * P)))
            tt(MSK0[0:NSAMP, 0, 2 * P:].rearrange("p (b t) -> p b t", t=NS),
               scs[:, PAST:].unsqueeze(1).broadcast_to([NSAMP, NB, NS]),
               c_("negblk")[0:NSAMP, NS:].rearrange("p (b t) -> p b t", t=NS), ALU.add).then_inc(sem("mask_done"), 1)

            def reduced(x, out):
                ch(red(out, x, AX.X, ALU.add))

            dve.wait_ge(sem("s3_in"), 16)
            with dve.Fori(0, 2) as t:
                ch.enter(t, 9)
                recurrence(tt, ch, t, S3, TB, SB, RP, RD, reduced)
            ch.leave(2)

            dve.sem_inc(sem("rope_out"), 2)
            with dve.Fori(0, HA) as i:
                ch.enter(i, 4)
                for s in range(2):
                    dve.wait_ge(sem("rope"), i * 2 + (s + 1))
                    dve.wait_ge(sem("rope_out"), i * 2 + (s + 2))
                    x = flat(QK[:, bass.ds(i * 2 + s, 1), :])
                    ch(tt(ROPT[:, 0, :], ps[6 + s][:, 0:NT], c_("sinA"), ALU.mult))
                    ch(tt(ROPT[:, 1, :], x, c_("cosA"), ALU.mult))
                    tt(x, ROPT[:, 0, :], ROPT[:, 1, :], ALU.add).then_inc(sem("rope_out"), 1)
            ch.leave(HA)
            dve.wait_ge(sem("rope_out"), 2 + 2 * HA)
            nc.vector.memset(ST, 0.0).then_inc(sem("state"), 1)
            ch(tt(AA, AA, bc(p_("lnx_b", 0, CT), full), ALU.add))

            def chunk(i, s):
                n = i * 4 + s
                dve.wait_ge(sem("turned"), n + 1)
                for q in range(4):
                    a, half = q % 2, q // 2
                    cp(BR[64 * a:64 * a + 64, half * 4:half * 4 + 4, :],
                       ps[4 + half][64 * a:64 * a + 64, :].rearrange("p (j a c) -> p j a c", a=2, c=64)[:, :, a, :]
                       ).then_inc(sem("br_out"), 1)
                dve.wait_ge(sem("x_done"), n + 1)
                cp(XS[64:64 + CH], ps[2][64:64 + CH, :].rearrange("p (h c) -> p h c", c=64)).then_inc(sem("x_out"), 1)
                dve.wait_ge(sem("u_done"), n + 1)
                cp(UV[64:64 + CH], ps[4][64:64 + CH, :].rearrange("p (h c) -> p h c", c=64)).then_inc(sem("u_out"), 1)
                dve.wait_ge(sem("chunk_done"), n + 2)
                ch(tt(ST, ST, ps[7][:, :].rearrange("p (j n) -> p j n", n=64), ALU.add))
                tt(ST, ST, PC[:, :, bass.ds(n, 1)].broadcast_to([P, CT, 64]), ALU.mult).then_inc(sem("state"), 1)

            with dve.Fori(0, 2) as i:
                ch.enter(i, 4 + 9)
                for s in range(4):
                    chunk(i, s)
                    if s == 1:
                        recurrence(tt, ch, i + 2, S3, TB, SB, RP, RD, reduced)
                        dve.sem_inc(sem("s3_done"), 1)
            ch.leave(2)

            for name, n in (("sbk_in", 32), ("sti_in", 32), ("sar_in", 16), ("sgr_in", 16)):
                dve.wait_ge(sem(name), n * (NCH + 1))
            dve.wait_ge(sem("sv_done"), 2 * (NCH + 1))

            def y_turn(n):
                if n == 0:
                    dve.wait_ge(sem("yT"), 1)
                    cp(YT[:, :, SEQ:NT], ps[1][:, 0:CT * NSAMP].rearrange("p (j n) -> p j n", n=NSAMP)).then_inc(
                        sem("yT_out"), 1)
                for j in range(4 * (n - 1), 4 * n):
                    if n in (1, 2):
                        dve.wait_ge(sem("mean"), j + 1)
                        stt(YD[:, j, :], ps[j % 2][:, 0:NT], -1.0 / DB, YT[:, j, :], ALU.mult, ALU.add).then_inc(
                            sem("mean_out"), 1)
                if n == 4:
                    dve.wait_ge(sem("y_sq"), 1)
                    ch(tt(YD, YD, bc(p_("lnx_w", 0, CT), full), ALU.mult))
                for j in range(4 * (n - 5), 4 * (n - 4)):
                    if n in (5, 6):
                        dve.wait_ge(sem("var"), j + 1)
                        ts(Y2[:, j, :], ps[j % 2][:, 0:NT], 1.0 / DB, LNX_EPS, ALU.mult, ALU.add).then_inc(
                            sem("var_out"), 1)
                for j in range(n - 8, n - 7):
                    if 0 <= j < CT:
                        dve.wait_ge(sem("var_root"), 1)
                        ch(nc.vector.reciprocal(Y2[:, j, :], Y2[:, j, :]))
                        if j % 2 == 1:
                            pair = slice(j - 1, j + 1)
                            ch(tt(YD[:, pair], YD[:, pair], Y2[:, pair], ALU.mult))
                            ch(tt(YD[:, pair], YD[:, pair], AA[:, pair], ALU.add))
                            tt(YT[:, pair], YD[:, pair], YT[:, pair], ALU.mult).then_inc(sem("ob_done"), 1)

            dve.wait_ge(sem("v_out"), 16)
            dve.wait_ge(sem("vrows"), 1)
            ch(cp(MSK[0:NSAMP], MSK0[0:NSAMP]))
            for n in range(2 * HA + 3):
                y_turn(n)
                if n == 3:
                    nc.vector.memset(QZ, 0.0).then_inc(sem("qz_zero"), 1)
                if n < 2 * HA:
                    dve.wait_ge(sem("ps_done"), n + 1)
                    if n >= 2:
                        dve.wait_ge(sem("pp_done"), n - 1)
                    stt(PS_[:, n % 2, :], ps[2 + n % 2][:, 0:SEQ], SCALE, MP[:, n // HA, :], ALU.mult,
                        ALU.add).then_inc(sem("ps_out"), 1)
                    dve.wait_ge(sem("ps_out"), n + 1)
                    red(ROWMAX[:, n % 2, :], PS_[:, n % 2, :], AX.X, ALU.max, negate=True).then_inc(sem("nmax"), 1)
                if 1 <= n <= 2 * HA:
                    m = n - 1
                    dve.wait_ge(sem("pexp"), m + 1)
                    ch(nc.vector.reciprocal(ROWSUM[:, m % 2, :], ROWSUM[:, m % 2, :]))
                    if m >= 2:
                        dve.wait_ge(sem("pt_done"), m - 1)
                    ts(PP[:, m % 2, :], PS_[:, m % 2, :], ROWSUM[:, m % 2, :], None, ALU.mult).then_inc(
                        sem("pp_done"), 1)
                if n >= 3:
                    m = n - 3
                    dve.wait_ge(sem("pv_prompt"), m + 1)
                    cp(OA[:, m % HA, (m // HA) * P:(m // HA + 1) * P], ps[6 + m % 2][:, 0:P]).then_inc(
                        sem("oa_prompt"), 1)

            dve.sem_inc(sem("oa_out"), 1)

            def select(b):
                tt(SEL[0:NSAMP], c_("dmask")[0:NSAMP], c_("oneseq")[0:NSAMP, bass.ds(b, 1)].broadcast_to(
                    [NSAMP, NSAMP]), ALU.mult).then_inc(sem("sel_done"), 1)

            select(0)
            with dve.Fori(0, NB) as b:
                ch.enter(b, 2)
                dve.wait_ge(sem("ss_done"), b + 1)
                red(MXC, ps[2][:, 0:2 * P + NSAMP], AX.X, ALU.max).then_inc(sem("mx_done"), 1)
                select(b + 1)
                dve.wait_ge(sem("mxT"), b + 1)
                red(NMR[0:1], ps[3][0:1, 0:P].rearrange("p (j n) -> p n j", n=NSAMP), AX.X, ALU.max,
                    negate=True).then_inc(sem("nm_done"), 1)
                dve.wait_ge(sem("mb"), b + 1)
                cp(NMX, ps[3][:, P:P + 1]).then_inc(sem("nmx_done"), 1)
                dve.wait_ge(sem("et_done"), b + 1)
                ch(cp(PTS[0:NSAMP, 2, 0:NSAMP], ps[4][0:NSAMP, 2 * P:2 * P + NSAMP]))
                cp(PTS[:, 0:2, :], ps[4][:, 0:2 * P].rearrange("p (a n) -> p a n", n=P)).then_inc(sem("pts_done"), 1)
                dve.wait_ge(sem("den"), b + 1)
                ch(nc.vector.reciprocal(RCP, ps[3][:, P + 1:P + 2]))
                tt(PICK, c_("pick"), RCP.broadcast_to([P, NSAMP]), ALU.mult).then_inc(sem("pick_done"), 1)
                dve.wait_ge(sem("pv_done"), b + 1)
                cp(OR[:, 0:512], ps[5][:, :]).then_inc(sem("or_done"), 1)
                dve.wait_ge(sem("os_done"), b + 1)
                cp(OA[:, :, bass.ds(b * NS + SEQ, NS)], ps[7][:, 0:NSAMP].rearrange("p (h t) -> p h t", t=NS)).then_inc(
                    sem("oa_out"), 1)
            ch.leave(NB)

            dve.sem_inc(sem("mix_free"), 2)
            with dve.Fori(0, KT // 2) as i:
                ch.enter(i, 4)
                for s in range(2):
                    n = i * 2 + s
                    dve.wait_ge(sem("gates"), i * 4 + 2 * (s + 1))
                    dve.wait_ge(sem("unit_read"), i * 4 + (U_MIX + 2 * s + 2))
                    ch(tt(T1[:, s, :], T1[:, s, :], ps[3 * s + 1][:, 0:NT], ALU.mult))
                    ch(tt(T2[:, s, :], SGB[:, s, :], ps[3 * s + 2][:, 0:NT], ALU.mult))
                    tt(flat(MIXT[:, bass.ds(n, 1), :]), T1[:, s, :], T2[:, s, :], ALU.add).then_inc(
                        sem("mix_free"), 1)
            ch.leave(KT // 2)

            dve.wait_ge(sem("x_again"), 16)
            dve.sem_inc(sem("o_free"), 2)
            with dve.Fori(0, KT // 4) as i:
                for s in range(4):
                    dve.wait_ge(sem("unit_read"), i * 4 + (U_O + s + 1))
                    x = flat(X1[:, bass.ds(i * 4 + s, 1), :])
                    tt(x, x, ps[s % 2][:, 0:NT], ALU.add).then_inc(sem("o_free"), 1)
            def low(u, n, at, m=KT * P):
                dve.wait_ge(sem("w_high"), n)
                raw = ring[:, u % 4].rearrange("p k c -> p (k c)")[:, 0:m]
                tt(W_LO[:, u % 4, 0:m], raw, W_HI[:, at, 0:m].bitcast(F32), ALU.subtract).then_inc(sem("w_split"), 1)

            low(U_FF, 1, 0)
            low(U_FF + 1, 2, 1)
            dve.wait_ge(sem("o_free"), 2 + KT)
            inv_rms(1)

            def h_low(g):
                dve.wait_ge(sem("h_high"), g + 1)
                tt(H_LO[:, 4 * g:4 * g + 4, 0:NT], hT[:, 4 * g:4 * g + 4, 0:NT],
                   H_HI[:, 4 * g:4 * g + 4, :].bitcast(F32), ALU.subtract).then_inc(sem("h_split"), 1)

            for k in range(KT):
                ins = normed(hT, X1, "g_ffn", k)
                if k % 4 == 3:
                    ins.then_inc(sem("h_done"), 1)
                else:
                    ch(ins)
                if k in (7, 11, 15):
                    h_low(k // 4 - 1)
            h_low(3)
            dve.wait_ge(sem("x1_out"), 16)

            dve.sem_inc(sem("ff_free"), 2)
            dve.sem_inc(sem("act_lo"), 2)
            def product(i, t, n=KT * P):
                low(U_FF + 2 * t + 2, i * 4 + (2 * t + 3), 0, n)
                low(U_FF + 2 * t + 3, i * 4 + (2 * t + 4), 1, n)
                dve.wait_ge(sem("silu"), i * 2 + (t + 1))
                dve.wait_ge(sem("act_lo"), i * 2 + (t + 1))
                dve.wait_ge(sem("unit_read"), i * 4 + (U_FF + 2 * t + 2))
                tt(UG[:, t, :], SIL[:, t, :], ps[2 * t + 1][:, 0:NT], ALU.mult).then_inc(sem("ff_free"), 1)
                dve.wait_ge(sem("act_high"), i * 2 + (t + 1))
                tt(flat(A_LO[:, bass.ds(i * 2 + t, 1), :]), UG[:, t, :],
                   flat(A_HI[:, bass.ds(i * 2 + t, 1), :]).bitcast(F32), ALU.subtract).then_inc(
                    sem("act_lo"), 1)

            with dve.Fori(0, FT // 2 - 1) as i:
                for t in range(2):
                    product(i, t)
            product(FT // 2 - 1, 0)
            product(FT // 2 - 1, 1, FQ * P)
            dve.sem_inc(sem("down_free"), 2)
            dve.wait_ge(sem("x1_in"), 16)
            with dve.Fori(0, KT // 2 - 1) as i:
                for t in range(2):
                    for q in range(4):
                        low(U_DOWN + q + 2, i * 8 + (2 * FT + 4 * t + q + 3), q % 2, FQ * P)
                    dve.wait_ge(sem("unit_read"), i * 8 + (U_DOWN + 4 * t + 4))
                    x = flat(XF[:, bass.ds(i * 2 + t, 1), :])
                    tt(x, x, ps[t][:, 0:NT], ALU.add).then_inc(sem("down_free"), 1)
            for t in range(2):
                for u in range(U_END - 8 + 4 * t, min(U_END - 4 + 4 * t, U_END - 2)):
                    low(u + 2, u + 3 - U_FF, u % 2 ^ 1, FQ * P)
                dve.wait_ge(sem("unit_read"), U_END - 4 + 4 * t)
                x = XF[:, KT - 2 + t, :]
                tt(x, x, ps[t][:, 0:NT], ALU.add).then_inc(sem("down_free"), 1)
            dve.wait_ge(sem("down_free"), 2 + KT)
            inv_rms(2)
            for k in range(KT):
                ins = normed(SQ2, XF, "g_final", k)
                if k < KT - 1:
                    ch(ins)
            ins.then_inc(sem("y_done"), 1)

        @block.gpsimd
        def _(pool):
            tt = nc.gpsimd.tensor_tensor
            ch = Chain(pool, "pool_chain")
            pool.wait_ge(sem("h_done"), 1)
            pool.dma_start(o_shift, LAST).then_inc(sem("shift_out"), 16)
            for a in range(6):
                pool.wait_ge(sem("rows_out"), 2 * (a + 1))
                pool.dma_start(rows_d[a], RW[0:NSAMP, a % 2, :]).then_inc(sem(f"rows_stored{a % 2}"), 16)
            pool.wait_ge(sem("arbk_done"), 1)
            for a, src in enumerate((ARt, BKt)):
                pool.dma_start(arbk_d[a].rearrange("c p n -> p c n"),
                               src.rearrange("p c j n -> p c (j n)")).then_inc(sem("arbk_stored"), 16)
            pool.wait_ge(sem("rope_idx_out"), 5)
            pool.dma_start(o_ki, KI[0:IDIM, :]).then_inc(sem("ki_out"), 16)
            for c in range(NCH):
                pool.wait_ge(sem("gram_out"), c + 1)
                pool.dma_start(gram_d[c], GS[:, c % 2, :]).then_inc(sem(f"gram_stored{c % 2}"), 16)

            def ki_pages(b, s):
                for p in range(NPG):
                    page = pool.value_load(ptab[0:1, bass.ds(b * NPG + p, 1)], min_val=0, max_val=POOL - 1)
                    pool.dma_start(KIB[:, s, p * P:(p + 1) * P], ki_d[bass.ds(page, 1)].rearrange(
                        "a p n -> p (a n)")).then_inc(sem(f"ki_in{s}"), 16)

            pool.wait_ge(sem("arbk_stored"), 32)
            pool.wait_ge(sem("const_in"), 64)
            ki_pages(0, 0)
            ki_pages(1, 1)
            for par in range(2):
                pool.wait_ge(sem(f"gram_stored{par}"), 16 * NCH // 2)
            for c in range(NCH):
                for a in range(2):
                    at = c * HB + a * CT
                    pool.dma_start(GL[at:at + CT], gram_d[c, 64 * a:64 * a + CH, :].rearrange(
                        "s (j t) -> j s t", t=64)[:, :, 0:CH]).then_inc(sem("gl_in"), 16)

            def store_scores(b):
                pool.wait_ge(sem("sc_out"), b + 2)
                pool.dma_start(sc_d[bass.ds(b * NS, NS), :], SC4[0:NS, :]).then_inc(sem("sc_stored"), 16)

            with pool.Fori(0, NB // 2 - 1) as i:
                for s in range(2):
                    store_scores(i * 2 + s)
                    ki_pages(i * 2 + (s + 2), s)
            store_scores(NB - 2)
            store_scores(NB - 1)
            pool.wait_ge(sem("sc_stored"), 16 * NB)
            pool.dma_start(SCS[0:NSAMP, :], sc_d[:, :]).then_inc(sem("scs_in"), 16)
            for par in range(2):
                pool.wait_ge(sem(f"rows_stored{par}"), 16 * 3)
            pool.wait_ge(sem("ki_out"), 16)
            for b in range(NB):
                for a in range(6):
                    pool.dma_start(SR[b * HB:(b + 1) * HB, a], rows_d[a, b * NS:(b + 1) * NS, :].rearrange(
                        "t (h j) -> h t j", j=DB)).then_inc(sem("sr_in"), 16)
            pool.wait_ge(sem("inv_done"), 1)
            for c in range(NCH):
                for a in range(2):
                    at = c * HB + a * CT
                    pool.dma_start(inv_d[c, a].rearrange("s j t -> j s t"), TI[at:at + CT]).then_inc(
                        sem("inv_stored"), 16)
            pool.wait_ge(sem("sr_in"), 16 * 6 * NB)

            def halve(x, out):
                w = DB // 2
                while w > 1:
                    ch(tt(x[:, :, 0:w], x[:, :, 0:w], x[:, :, w:2 * w], ALU.add))
                    w //= 2
                ch(tt(out, x[:, :, 0:1], x[:, :, 1:2], ALU.add))

            pool.dma_start(S3, wkv_d[:, RP:, :]).then_inc(sem("s3_in"), 16)
            pool.dma_start(S2, wkv_d[:, 0:RP, :]).then_inc(sem("s2_in"), 16)
            pool.wait_ge(sem("s2_in"), 16)
            with pool.Fori(0, NS) as t:
                ch.enter(t, 19)
                recurrence(tt, ch, t, S2, TA, SA, 0, RP, halve)
            ch.leave(NS)
            pool.dma_start(o_wkvs[:, 0:RP, :], S2).then_inc(sem("wkvs_out"), 16)
            pool.wait_ge(sem("wkvs_out"), 16)
            pool.dma_start(G2[:, 0, :], lora_d[1]).then_inc(sem("g2_in"), 16)
            pool.dma_start(G2[0:32, 1, :], lora_d[2, 0:32]).then_inc(sem("g2_in"), 16)
            pool.wait_ge(sem("s3_done"), 2)
            pool.dma_start(o_wkvs[:, RP:, :], S3).then_inc(sem("wkvs_out"), 16)
            for b in range(NB):
                pool.dma_start(yrow_d[b * NS:(b + 1) * NS, :].rearrange("t (h j) -> h t j", j=DB),
                               SY[b * HB:(b + 1) * HB]).then_inc(sem("yrow_stored"), 16)
            pool.wait_ge(sem("yrow_stored"), 16 * NB)
            pool.wait_ge(sem("rope_out"), 2 + 2 * HA)
            pool.dma_start(YR[0:NSAMP], yrow_d[:, :]).then_inc(sem("yrow_in"), 16)
            pool.wait_ge(sem("state"), NCH + 1)
            pool.dma_start(o_wkv, ST).then_inc(sem("wkv_out"), 16)
            pool.wait_ge(sem("oa_out"), NB + 1)
            pool.wait_ge(sem("qb_done"), NB + 1)
            pool.dma_start(XR, xT[:, :, 0:NT]).then_inc(sem("x_again"), 16)
            pool.wait_ge(sem("o_free"), 2 + KT)
            pool.dma_start(x1_d[:, :, :], X1).then_inc(sem("x1_out"), 16)
            pool.wait_ge(sem("x1_out"), 16)
            pool.wait_ge(sem("unit_read"), U_DOWN)
            pool.dma_start(XF, x1_d[:, :, :]).then_inc(sem("x1_in"), 16)


def kernel(**inputs):
    import concourse.bacc as _bacc
    from concourse.bass_utils import run_bass_kernel_spmd as _run

    a = {k: np.asarray(v) for k, v in inputs.items()}
    f32 = np.float32

    def tiles_of(w):
        k, n = w.shape
        return w.reshape(k // P, P, n // P, P).transpose(2, 1, 0, 3).reshape(n // P, P, -1)

    def cols(v):
        return v.reshape(-1, P).T

    w_in = a["w_in"][0]
    n_in_a = w_in.shape[1] - 3360
    wa, wb = w_in[:, :n_in_a], w_in[:, n_in_a:]

    def padded(w, n):
        return np.concatenate([w, np.zeros((w.shape[0], n - w.shape[1]), f32)], 1)

    small = padded(wb[:, 3072:], 3 * P)
    ki, wi = wa[:, 3584:3648], wa[:, 3648:3656]
    idx = np.concatenate([wa[:, 3072:3584], ki, ki, padded(wi, P)], 1)
    ga, gb = wa[:, 3656:5704], wa[:, 5704:]
    pa, pb = tiles_of(a["w_pa"][0]), tiles_of(a["w_pb"][0])
    mixu = np.stack([tiles_of(gb), np.concatenate([pa, pb], 2)], 1).reshape(2 * KT, P, -1)
    ffu = np.stack([tiles_of(a["w_gate"][0]), tiles_of(a["w_up"][0])], 1).reshape(2 * FT, P, -1)
    wst = np.concatenate([tiles_of(small), tiles_of(wb[:, :3072]), tiles_of(idx), tiles_of(wa[:, :3072]), tiles_of(ga),
                          mixu, tiles_of(a["w_o"][0]), ffu], 0)
    wd = a["w_down"][0].reshape(4, FQ, P, KT, P).transpose(3, 0, 2, 1, 4).reshape(4 * KT, P, FQ * P)
    x = np.concatenate([a["x_prompt"][0], a["x_sample"].reshape(NSAMP, DM), a["state_shift"][0]], 0)
    xT = x.T.reshape(KT, P, NX).transpose(1, 0, 2)
    mu = a["mu_b"][0]
    mu = np.concatenate([mu[3072:], np.zeros(3 * P - 288, f32), mu[:3072]])
    prm = np.concatenate([cols(a["g_mix"]), cols(a["g_ffn"]), cols(a["g_final"]), cols(mu)]
                         + [cols(a[n]) for n in ("w0", "a0", "k_k", "k_a", "r_k", "lnx_w", "lnx_b")], 1)
    g2 = a["g2"][0]
    lora = np.stack([np.concatenate([a["w2"][0], a["a2"][0]], 0), g2[:P],
                     np.concatenate([g2[P:], np.zeros((2 * P - 160, 1024), f32)], 0)], 0)
    kT = a["cache_k"][0].transpose(0, 3, 2, 1).reshape(POOL, P, HA * P)
    vc = a["cache_v"][0].reshape(POOL, P, HA * P)
    kic = a["cache_kidx"][0].transpose(0, 2, 1)
    kic = np.concatenate([kic, kic], 1)
    wkv = a["state_wkv"][0].reshape(NB * HB, DB, DB)
    ins = dict(wst=wst, wdn=wd, xT=xT, cst=constants(), prm=prm, lora=lora, kT=kT, v=vc, ki=kic, wkv=wkv,
               pt=a["page_table"].reshape(1, -1))
    outs = dict(y=(P, KT, NT), k=(P, HA, NT), v=(P, HA, NT), ki=(IDIM, NT), wkv=(P, CT, DB), shift=(P, KT, 1 + NB),
                wkvs=(P, DB, DB))

    nc = _bacc.Bacc("TRN2", target_bir_lowering=False, num_devices=1)
    arrays, args = {}, []
    for name, v in ins.items():
        v = np.ascontiguousarray(v)
        arrays[f"in_{name}"] = v
        args.append(nc.dram_tensor(f"in_{name}", v.shape, mybir.dt.from_np(v.dtype), kind="ExternalInput").ap())
    for name, shape in outs.items():
        args.append(nc.dram_tensor(f"out_{name}", shape, F32, kind="ExternalOutput").ap())
    program(nc, *args)
    r = _run(nc, [arrays], core_ids=[0]).results[0]
    o = {n: np.asarray(r[f"out_{n}"]) for n in outs}

    y = o["y"].transpose(2, 1, 0).reshape(NT, DM)
    k, v = (o[n].transpose(2, 1, 0) for n in ("k", "v"))
    ki = o["ki"].T
    wkvp = o["wkv"].reshape(2, DB, CT, DB).transpose(2, 0, 3, 1).reshape(1, 1, HB, DB, DB)
    sh = o["shift"].transpose(2, 1, 0).reshape(1 + NB, DM)
    return (y[:SEQ].reshape(1, SEQ, DM), y[SEQ:].reshape(NB, NS, DM),
            k[:SEQ].reshape(1, 1, SEQ, HA, DH), v[:SEQ].reshape(1, 1, SEQ, HA, DH), ki[:SEQ].reshape(1, 1, SEQ, IDIM),
            wkvp, sh[:1].reshape(1, 1, DM),
            k[SEQ:].reshape(1, NB, NS, HA, DH), v[SEQ:].reshape(1, NB, NS, HA, DH),
            ki[SEQ:].reshape(1, NB, NS, IDIM), o["wkvs"].reshape(1, NB, HB, DB, DB), sh[1:].reshape(1, NB, DM))
```
